# Optimizing a Trainium2 kernel written in Bass

```python
import jax, jax.numpy as jnp
from jax import lax
import numpy as np

D_MODEL = 1024
BATCH = 1
SEQ = 512
DEPTH = 2

N_MIXERS = 2
N_A = (DEPTH + 1) // 2
N_B = DEPTH // 2
HG_EXPAND = 128
HG_HEADS = D_MODEL // 128
HG_FDIM = HG_HEADS * HG_EXPAND
HG_VDIM = D_MODEL // HG_HEADS
HG_CHUNK = 64
FOX_HEAD_DIM = 64
FOX_HEADS = D_MODEL // FOX_HEAD_DIM
FOX_BLOCK = 128
D_FF = 4 * D_MODEL
N_MOD = 6
EPS = 1e-6

kernel_name = "hybrid_hgrn2_fox_adaln_block"

def rmsnorm(x, w):
    xf = x.astype(jnp.float32)
    y = xf * lax.rsqrt(jnp.mean(xf * xf, axis=-1, keepdims=True) + EPS)
    return (y * w.astype(jnp.float32)).astype(x.dtype)

def modulate(x, w, shift, scale):
    return rmsnorm(x, w) * (1 + scale[:, None, :]) + shift[:, None, :]

def hgrn2_mixer(h, w_in, w_out, lb, gn_w):
    B, S, _ = h.shape
    H, dk, dv, C = HG_HEADS, HG_EXPAND, HG_VDIM, HG_CHUNK
    N = S // C
    proj = h @ w_in
    q, fz, i, g = jnp.split(proj, [HG_FDIM, 2 * HG_FDIM, 2 * HG_FDIM + D_MODEL], axis=-1)
    q = jax.nn.silu(q.astype(jnp.float32))
    lbf = lb.astype(jnp.float32)
    logf = jnp.logaddexp(jnp.log(lbf), jnp.log1p(-lbf) + jax.nn.log_sigmoid(fz.astype(jnp.float32)))
    k = -jnp.expm1(logf)
    v = i.astype(jnp.float32)

    def to_chunks(t, d):
        return t.reshape(B, N, C, H, d).transpose(1, 0, 3, 2, 4)

    qc, kc, gc, vc = to_chunks(q, dk), to_chunks(k, dk), to_chunks(logf, dk), to_chunks(v, dv)
    causal = jnp.tril(jnp.ones((C, C), dtype=bool))

    def step(state, inp):
        qb, kb, gb, vb = inp
        G = jnp.cumsum(gb, axis=2)
        diff = G[:, :, :, None, :] - G[:, :, None, :, :]
        decay = jnp.exp(jnp.where(causal[:, :, None], diff, -jnp.inf))
        A = jnp.einsum('bhtk,bhsk,bhtsk->bhts', qb, kb, decay)
        o = jnp.einsum('bhts,bhsv->bhtv', A, vb) + jnp.einsum('bhtk,bhkv->bhtv', qb * jnp.exp(G), state)
        G_last = G[:, :, -1:, :]
        new_state = jnp.exp(G_last[:, :, 0, :])[..., None] * state + \
            jnp.einsum('bhsk,bhsv->bhkv', kb * jnp.exp(G_last - G), vb)
        return new_state, o

    state0 = jnp.zeros((B, H, dk, dv), jnp.float32)
    _, o = lax.scan(step, state0, (qc, kc, gc, vc))
    o = o.transpose(1, 0, 3, 2, 4).reshape(B, S, H, dv)
    o = rmsnorm(o, gn_w).reshape(B, S, D_MODEL)
    o = (o * jax.nn.silu(g.astype(jnp.float32))).astype(h.dtype)
    return o @ w_out

def fox_mixer(h, w_in, b_f, qn_w, kn_w, w_out):
    B, S, _ = h.shape
    H, dh, blk = FOX_HEADS, FOX_HEAD_DIM, FOX_BLOCK
    proj = h @ w_in
    q, k, v, g, fz = jnp.split(proj, [D_MODEL, 2 * D_MODEL, 3 * D_MODEL, 4 * D_MODEL], axis=-1)
    q = rmsnorm(q.reshape(B, S, H, dh), qn_w).transpose(0, 2, 1, 3)
    k = rmsnorm(k.reshape(B, S, H, dh), kn_w).transpose(0, 2, 1, 3)
    v = v.reshape(B, S, H, dh).transpose(0, 2, 1, 3)
    logf = jax.nn.log_sigmoid(fz.astype(jnp.float32) + b_f.astype(jnp.float32))
    F = jnp.cumsum(logf, axis=1).transpose(0, 2, 1)
    scale = 1.0 / np.sqrt(dh)
    kpos = jnp.arange(S)

    def block(bi):
        start = bi * blk
        qb = lax.dynamic_slice_in_dim(q, start, blk, axis=2)
        Fq = lax.dynamic_slice_in_dim(F, start, blk, axis=2)
        s = jnp.einsum('bhqd,bhkd->bhqk', qb, k).astype(jnp.float32) * scale
        s = s + (Fq[..., :, None] - F[..., None, :])
        qpos = start + jnp.arange(blk)
        s = jnp.where(kpos[None, :] <= qpos[:, None], s, -jnp.inf)
        p = jax.nn.softmax(s, axis=-1)
        return jnp.einsum('bhqk,bhkd->bhqd', p.astype(v.dtype), v)

    o = lax.map(block, jnp.arange(S // blk))
    o = o.transpose(1, 0, 3, 2, 4).reshape(B, S, D_MODEL)
    o = o * jax.nn.sigmoid(g)
    return o @ w_out

def sqrelu_mlp(h, w1, w2):
    a = jax.nn.relu(h @ w1)
    return (a * a) @ w2

def setup_inputs(seed: int = 0) -> dict:
    key = jax.random.key(seed)
    ks = jax.random.split(key, 20)
    D, F = D_MODEL, HG_FDIM
    nrm = jax.random.normal
    return {
        "x": nrm(ks[0], (BATCH, SEQ, D), jnp.float32),
        "c": nrm(ks[1], (BATCH, D), jnp.float32),
        "w_mod": nrm(ks[2], (DEPTH, D, N_MOD * D), jnp.float32) * (0.5 * D ** -0.5),
        "b_mod": nrm(ks[3], (DEPTH, N_MOD * D), jnp.float32) * 0.02,
        "norm1_w": 1.0 + 0.05 * nrm(ks[4], (DEPTH, D), jnp.float32),
        "norm2_w": 1.0 + 0.05 * nrm(ks[5], (DEPTH, D), jnp.float32),
        "hg_w_in": nrm(ks[6], (N_A, D, 2 * F + 2 * D), jnp.float32) * D ** -0.5,
        "hg_w_out": nrm(ks[7], (N_A, D, D), jnp.float32) * D ** -0.5,
        "hg_lb": 0.5 * nrm(ks[8], (DEPTH + 1, F), jnp.float32),
        "hg_gn_w": 1.0 + 0.05 * nrm(ks[9], (N_A, HG_VDIM), jnp.float32),
        "fox_w_in": nrm(ks[10], (N_B, D, 4 * D + FOX_HEADS), jnp.float32) * D ** -0.5,
        "fox_b_f": jax.random.uniform(ks[11], (N_B, FOX_HEADS), jnp.float32, 1.0, 4.0),
        "fox_qn_w": 1.0 + 0.05 * nrm(ks[12], (N_B, FOX_HEAD_DIM), jnp.float32),
        "fox_kn_w": 1.0 + 0.05 * nrm(ks[13], (N_B, FOX_HEAD_DIM), jnp.float32),
        "fox_w_out": nrm(ks[14], (N_B, D, D), jnp.float32) * D ** -0.5,
        "mlp_w1": nrm(ks[15], (DEPTH, D, D_FF), jnp.float32) * D ** -0.5,
        "mlp_w2": nrm(ks[16], (DEPTH, D_FF, D), jnp.float32) * D_FF ** -0.5,
        "final_w": 1.0 + 0.05 * nrm(ks[17], (D,), jnp.float32),
    }

def reference(x, c, w_mod, b_mod, norm1_w, norm2_w, hg_w_in, hg_w_out, hg_lb, hg_gn_w,
              fox_w_in, fox_b_f, fox_qn_w, fox_kn_w, fox_w_out, mlp_w1, mlp_w2, final_w):
    lb_all = jnp.cumsum(jax.nn.softmax(hg_lb.astype(jnp.float32), axis=0), axis=0)
    c_act = jax.nn.silu(c)
    for i in range(DEPTH):
        mod = c_act @ w_mod[i] + b_mod[i]
        sh1, sc1, g1, sh2, sc2, g2 = jnp.split(mod, N_MOD, axis=-1)
        h = modulate(x, norm1_w[i], sh1, sc1)
        j = i // N_MIXERS
        if i % N_MIXERS == 0:
            y = hgrn2_mixer(h, hg_w_in[j], hg_w_out[j], lb_all[i], hg_gn_w[j])
        else:
            y = fox_mixer(h, fox_w_in[j], fox_b_f[j], fox_qn_w[j], fox_kn_w[j], fox_w_out[j])
        x = x + g1[:, None, :] * y
        h = modulate(x, norm2_w[i], sh2, sc2)
        x = x + g2[:, None, :] * sqrelu_mlp(h, mlp_w1[i], mlp_w2[i])
    return rmsnorm(x, final_w)


_drawn_inputs = setup_inputs


def setup_inputs(seed=0):
    import zlib

    import numpy as np

    out = dict(_drawn_inputs(seed))
    spreads = {}
    factors = {'norm1_w': 3.949,
     'hg_lb': 8.0,
     'hg_gn_w': 4.854,
     'fox_qn_w': 21.494,
     'fox_kn_w': 8.0,
     'norm2_w': 4.5}
    for name, (base, spread) in spreads.items():
        noise = np.random.default_rng([zlib.crc32(name.encode()), seed]).standard_normal(out[name].shape)
        drawn = base * np.exp(spread * noise) if base else spread * noise
        out[name] = __import__('jax').numpy.asarray(drawn.astype(out[name].dtype))
    for name, factor in factors.items():
        out[name] = (out[name] * factor).astype(out[name].dtype)
    return out
```

```python
import numpy as np
import concourse.bass as bass
import concourse.mybir as mybir
from concourse.alu_op_type import AluOpType as ALU
from contextlib import ExitStack

F32 = mybir.dt.float32
F32R = mybir.dt.float32r
BF16 = mybir.dt.bfloat16
U8 = mybir.dt.uint8
ACT = mybir.ActivationFunctionType
AX = mybir.AxisListType

P = 128
T = 512
TT = T // P
D = 1024
KT = D // P
EPS = 1e-6
HEADS = 16
DH = 64
GH = 4
FH = 8
FF = 4 * D
HALF = FF // 2 // P

Q_IN, Q_OUT, Q_MLP = 0, 8, 10
LAYER_QUADS = 26
QUADS = 2 * LAYER_QUADS

C_N1, C_N2, C_FIN, C_LB, C_GN, C_QN, C_KN, C_BF, C_BMOD = 0, 16, 32, 40, 64, 65, 66, 67, 68
C_ALL = C_BMOD + 96
SH1, SC1, G1, SH2, SC2, G2 = (8 * i for i in range(6))

MASKED = 8
SPLITS = 10


def build(nc, x_t, c_row, stream, mod_rows, w_forget, params, out_t):
    keep = ExitStack()
    with keep:
        def sem(name):
            return keep.enter_context(nc.semaphore(name))

        def sb(name, shape, dt, ctx=keep):
            return ctx.enter_context(nc.sbuf_tensor(name, shape, dt))

        x = sb("x", [P, KT, T], F32)
        raw = sb("raw", [P, 4, D], F32)
        whi = sb("whi", [P, 4, D], F32R)
        wlo = sb("wlo", [P, 4, D], F32R)
        par = sb("par", [P, C_ALL], F32)
        mod = sb("mod", [P, 96], F32)
        gain = sb("gain", [P, 4 * KT], F32)
        small = sb("small", [P, 64], F32)
        dots = sb("dots", [P, 4], F32)
        qkw = sb("qkw", [P, 1], F32)
        ident = sb("ident", [P, P], F32)
        identb = sb("identb", [P, P], BF16)
        causal = sb("causal", [P, P], BF16)
        ones = sb("ones", [P, P], F32)
        mhalf = sb("mhalf", [P, 32], F32)
        ssq = sb("ssq", [P, 64], F32)
        rst = sb("rst", [P, 64], F32)
        meand = sb("meand", [P, 2], F32)
        scr = [sb(f"scr{i}", [P, T], F32) for i in range(2)]
        sqb = sb("sqb", [P, T], F32)
        acc = sb("acc", [P, T], F32)

        layer0 = ExitStack()
        mring = sb("mring", [P, 2, D], F32, layer0)
        cb = sb("cb", [P, D], F32, layer0)
        masks = sb("masks", [P, MASKED, P], U8, layer0)
        lbc = sb("lbc", [P, 6 * KT], F32, layer0)

        head0 = ExitStack()
        modf = sb("modf", [P, 16, D], F32, head0)
        head0.close()
        hg = ExitStack()
        hq, hk, hf, hg_ = (sb(n, [P, GH, T], F32, hg) for n in ("hq", "hk", "hf", "hgate"))
        hv = sb("hv", [P, TT, T], F32, hg)
        adiag = sb("adiag", [P, GH, T], F32, hg)
        h0 = [sb(n, [P, KT, T], F32R, hg) for n in ("h0hi", "h0lo")]
        y0 = [sb(n, [P, KT, T], F32R, hg) for n in ("y0hi", "y0lo")]
        hg.close()
        mlp0 = ExitStack()
        a0 = [sb(n, [P, HALF, T], F32R, mlp0) for n in ("a0hi", "a0lo")]
        h1 = [sb(n, [P, KT, T], F32R, mlp0) for n in ("h1hi", "h1lo")]
        wf = sb("wf", [P, D], F32, mlp0)
        wfs = [sb(n, [P, D], F32R, mlp0) for n in ("wfhi", "wflo")]
        mlp0.close()
        layer0.close()
        fox = ExitStack()
        qt, kt_, vt = (sb(n, [P, TT, T], F32, fox) for n in ("qt", "kt", "vt"))
        gs, qT, kT = (sb(n, [P, 4, T], F32, fox) for n in ("gs", "qT", "kT"))
        pT = sb("pT", [P, 2, T], F32, fox)
        fb = sb("fb", [P, FH, T], F32, fox)
        h2 = [sb(n, [P, KT, T], F32R, fox) for n in ("h2hi", "h2lo")]
        y1 = [sb(n, [P, KT, T], F32R, fox) for n in ("y1hi", "y1lo")]
        fox.close()
        mlp1 = ExitStack()
        a1 = [sb(n, [P, HALF, T], F32R, mlp1) for n in ("a1hi", "a1lo")]
        h3 = [sb(n, [P, KT, T], F32R, mlp1) for n in ("h3hi", "h3lo")]
        mlp1.close()
        fscr = nc.dram_tensor("negf", [HEADS, T], F32).ap()

        ps = [keep.enter_context(nc.psum_tensor(f"bank{i}", [P, T], F32)) for i in range(8)]

        raw_in = [sem(f"raw_in{i}") for i in range(4)]
        w_hi, w_lo = sem("w_hi"), sem("w_lo")
        pe_blk = sem("pe_blk")
        x_in, par_in, wf_in, c_in = (sem(n) for n in ("x_in", "par_in", "wf_in", "c_in"))
        modf_in = [sem(f"modf_in{i}") for i in range(4)]
        mod_in = [sem(f"mod_in{i}") for i in range(2)]
        mod_used = sem("mod_used")
        mod_set = sem("mod_set")
        consts = sem("consts")
        cact = sem("cact")
        dv = sem("dv")
        gp = sem("gp")
        ac = sem("ac")
        lb_mx, lb_ex = sem("lb_mx"), sem("lb_ex")
        x_sq, x_upd = sem("x_sq"), sem("x_upd")
        x_acc = sem("x_acc")
        n_sum, n_var, n_rst, n_dg, n_bc = (sem(n) for n in ("n_sum", "n_var", "n_rst", "n_dg", "n_bc"))
        h_t, h_hi, h_lo = (sem(n) for n in ("h_t", "h_hi", "h_lo"))
        ev = sem("ev")
        kf = sem("kf")
        lvl, sel, qup, kup = (sem(n) for n in ("lvl", "sel", "qup", "kup"))
        off, o_pe, o_ev = (sem(n) for n in ("off", "o_pe", "o_ev"))
        g_sum, g_var, g_rst, g_dg, g_bc = (sem(n) for n in ("g_sum", "g_var", "g_rst", "g_dg", "g_bc"))
        y_t, y_hi, y_lo = (sem(n) for n in ("y_t", "y_hi", "y_lo"))
        ff_r, ff_sq, ff_hi, ff_lo = (sem(n) for n in ("ff_r", "ff_sq", "ff_hi", "ff_lo"))
        f_w, f_wl, f_pe, f_abs, f_ln, f_out, f_dram, f_bc = (
            sem(n) for n in ("f_w", "f_wl", "f_pe", "f_abs", "f_ln", "f_out", "f_dram", "f_bc"))
        fev, fsq, fss = sem("fev"), sem("fsq"), sem("fss")
        f_var, f_rst, f_nrm, f_tr, f_te = (sem(n) for n in ("f_var", "f_rst", "f_nrm", "f_tr", "f_te"))
        s_pe, s_ns, s_p, s_tr, s_pt, s_pv, s_o = (
            sem(n) for n in ("s_pe", "s_ns", "s_p", "s_tr", "s_pt", "s_pv", "s_o"))
        ot_tr = sem("ot_tr")
        fy_t, fy_hi, fy_lo = (sem(n) for n in ("fy_t", "fy_hi", "fy_lo"))
        out_t_ready, out_done = sem("out_t_ready"), sem("out_done")

        NORM_SQ = [1, 2, 4, 5, 7]
        UPD = [0, KT, 3 * KT, 4 * KT]
        DG = [sqb, acc]
        UNITS = FH * TT
        V, S, G, PE = nc.vector, nc.scalar, nc.gpsimd, nc.tensor

        def tile(t, i):
            return t[:, bass.ds(i, 1), :].rearrange("p o n -> p (o n)")

        def col(t, i):
            return t[:, bass.ds(i, 1)]

        def cols(t, i):
            return t[:, P * i:P * (i + 1)]

        block = keep.enter_context(nc.Block())

        @block.sync
        def _(sp):
            sp.dma_start(par[:, :], params).then_inc(par_in, 16)
            sp.dma_start(cb[:, :], c_row.partition_broadcast(P)).then_inc(c_in, 16)
            for i in range(4):
                sp.dma_start(modf[:, 4 * i:4 * i + 4, :],
                             mod_rows[4 * i:4 * i + 4].rearrange("m p k -> p m k")).then_inc(modf_in[i], 16)
            sp.dma_start(x[:, :, :], x_t).then_inc(x_in, 16)

            def weight(quad, j):
                sp.dma_start(raw[:, j, :], stream[bass.ds(quad * 4 + j, 1)].rearrange("b p n -> (b p) n")
                             ).then_inc(raw_in[j], 16)

            def modulation(m, s):
                sp.wait_ge(mod_used, m - 1)
                sp.dma_start(mring[:, s, :], mod_rows[bass.ds(m + 16, 1)].rearrange("b p n -> (b p) n")
                             ).then_inc(mod_in[s], 16)

            for j in range(4):
                weight(0, j)
            for j in range(4):
                sp.wait_ge(w_lo, j + 1)
                weight(1, j)
            for j in range(4):
                sp.wait_ge(w_lo, 4 + j + 1)
                weight(2, j)
                if j < 2:
                    sp.dma_start(mring[:, j, :], mod_rows[16 + j]).then_inc(mod_in[j], 16)
                else:
                    modulation(j, j % 2)
            with sp.Fori(3, 10) as q:
                for j in range(4):
                    sp.wait_ge(w_lo, (q - 1) * 4 + j + 1)
                    weight(q, j)
                    modulation((q - 2) * 4 + j, j % 2)
            with sp.Fori(10, 12) as q:
                for j in range(4):
                    sp.wait_ge(w_lo, (q - 1) * 4 + j + 1)
                    weight(q, j)
            with sp.Fori(12, 24) as q:
                for j in range(4):
                    sp.wait_ge(w_lo, (q - 1) * 4 + j + 1)
                    weight(q, j)
                    modulation((q - 4) * 4 + j, j % 2)
            sp.dma_start(wf[:, :], w_forget).then_inc(wf_in, 16)
            with sp.Fori(24, QUADS) as q:
                for j in range(4):
                    sp.wait_ge(w_lo, (q - 1) * 4 + j + 1)
                    weight(q, j)
            for k in range(KT):
                sp.wait_ge(out_t_ready, k + 1)
                sp.dma_start(out_t[:, k, :], x[:, k, :]).then_inc(out_done, 16)
            sp.wait_ge(out_done, 16 * KT)

        @block.scalar
        def _(act):
            def hi_ahead(quad, j):
                act.wait_ge(pe_blk, quad * 4 + j + 1)
                act.wait_ge(raw_in[j], quad * 16 + 32)
                S.activation(whi[:, j, :], raw[:, j, :], ACT.Copy).then_inc(w_hi, 1)

            def norm(n, h, shift, first=False):
                for k in range(KT):
                    act.wait_ge(h_t, n * KT + k + 1)
                    S.activation(h[0][:, k, :], scr[k % 2][:, :], ACT.Identity,
                                 bias=mod[:, shift + k:shift + k + 1]).then_inc(h_hi, 1)

            act.wait_ge(c_in, 16)
            S.activation(cb[:, :], cb[:, :], ACT.Silu).then_inc(cact, 1)
            act.wait_ge(lb_mx, 1)
            S.activation(lbc[:, 24:48], lbc[:, 0:24], ACT.Exp).then_inc(lb_ex, 1)
            for j in range(4):
                act.wait_ge(raw_in[j], 16)
                S.activation(whi[:, j, :], raw[:, j, :], ACT.Copy).then_inc(w_hi, 1)
            act.wait_ge(consts, 1)
            act.wait_ge(x_in, 16)
            for k in range(KT):
                if k:
                    act.wait_ge(x_acc, k)
                S.activation(sqb[:, :], x[:, k, :], ACT.Square).then_inc(x_sq, 1)
            norm(0, h0, SH1)

            with act.Fori(0, 2) as g:
                q0 = g * 4
                for j in range(4):
                    act.wait_ge(pe_blk, q0 * 4 + j + 1)
                    act.wait_ge(y_t, g * 4)
                    S.activation(hq[:, j, :], ps[j][:, :], ACT.Silu).then_inc(ev, 1)
                    hi_ahead(q0, j)
                for j in range(4):
                    act.wait_ge(pe_blk, q0 * 4 + 4 + j + 1)
                    S.activation(hf[:, j, :], ps[4 + j][:, :], ACT.Sigmoid)
                    S.activation(hk[:, j, :], ps[4 + j][:, :], ACT.Sigmoid, scale=-1.0).then_inc(ev, 1)
                    hi_ahead(q0 + 1, j)
                for j in range(3):
                    hi_ahead(q0 + 2, j)
                act.wait_ge(pe_blk, q0 * 4 + 12)
                for t in range(TT):
                    S.activation(hv[:, t, :], ps[t][:, :], ACT.Copy).then_inc(ev, 1)
                hi_ahead(q0 + 2, 3)
                for j in range(4):
                    act.wait_ge(pe_blk, q0 * 4 + 12 + j + 1)
                    S.activation(hg_[:, j, :], ps[4 + j % 2][:, :], ACT.Silu).then_inc(ev, 1)
                    hi_ahead(q0 + 3, j)
                for j in range(GH):
                    act.wait_ge(lvl, g * 40 + 36 + (j | 1) + 1)
                    S.activation(hf[:, j, :], ps[j][:, :], ACT.Copy)
                    S.activation(hk[:, j, 256:512], ps[6 + j // 2][:, 256 * (j % 2):256 * (j % 2) + 256],
                                 ACT.Copy).then_inc(off, 1)
                for j in range(GH):
                    act.wait_ge(o_pe, g * 4 + j + 1)
                    S.activation(hq[:, j, :], ps[4 + j % 2][:, :], ACT.Copy)
                    S.activation(hk[:, j, :], ps[4 + j % 2][:, :], ACT.Square).then_inc(o_ev, 1)
                for j in range(GH):
                    act.wait_ge(y_t, g * 4 + j + 1)
                    S.activation(tile(y0[0], g * 4 + j), scr[j % 2][:, :], ACT.Copy).then_inc(y_hi, 1)

            def residual(quads, q0, per, sq0, first):
                def body(q, last):
                    for j in range(4):
                        if not last:
                            hi_ahead(q0 + q, j)
                        if j % per == per - 1:
                            n = q * (4 // per) + j // per
                            act.wait_ge(x_upd, sq0 + n + 1)
                            act.wait_ge(x_acc, sq0 + n + KT)
                            S.activation(sqb[:, :], tile(x, n), ACT.Square).then_inc(x_sq, 1)
                n_loop = quads - (1 if first else 0)
                with act.Fori(0, n_loop) as q:
                    body(q, False)
                if first:
                    body(quads - 1, True)

            def mlp(layer, a, n_norm, h, sq0):
                base = layer * LAYER_QUADS + Q_MLP
                for half in range(2):
                    with act.Fori(0, 4) as q:
                        for j in range(4):
                            act.wait_ge(pe_blk, (q + base + 8 * half) * 4 + j + 1)
                            ff_n = (q + 4 * half) * 4 + j + 32 * layer
                            if layer or half or j >= 2:
                                act.wait_ge(ff_lo, ff_n - 1)
                            S.activation(scr[j % 2][:, :], ps[j][:, :], ACT.Relu).then_inc(ff_r, 1)
                            hi_ahead(q + base + 8 * half, j)
                            act.wait_ge(ff_sq, ff_n + 1)
                            S.activation(tile(a[0], q * 4 + j), scr[j % 2][:, :], ACT.Copy).then_inc(ff_hi, 1)
                    residual(4, base + 8 * half + 4, 2, sq0 + KT * half, layer == 1 and half == 1)

            residual(2, Q_OUT, 1, 0, False)
            norm(1, h1, SH2)
            mlp(0, a0, 1, h1, KT)
            act.wait_ge(wf_in, 16)
            S.activation(wfs[0][:, :], wf[:, :], ACT.Copy).then_inc(f_w, 1)
            norm(2, h2, 48 + SH1)
            act.wait_ge(f_pe, 1)
            S.activation(sqb[:, :], ps[0][:, :], ACT.Abs, bias=par[:, C_BF:C_BF + 1]).then_inc(ac, 1)
            act.wait_ge(ac, 1)
            S.activation(sqb[:, :], sqb[:, :], ACT.Exp, scale=-1.0).then_inc(ac, 1)
            act.wait_ge(ac, 2)
            S.activation(sqb[:, :], sqb[:, :], ACT.Ln, bias=1.0).then_inc(f_ln, 1)
            act.wait_ge(f_out, 1)
            act.dma_start(fscr, acc[0:HEADS, :]).then_inc(f_dram, 16)
            act.wait_ge(f_dram, 16)

            L = LAYER_QUADS
            with act.Fori(0, 2) as g:
                q0 = g * 4 + L
                act.wait_ge(s_ns, g * UNITS)
                act.dma_start(fb[:, :, :], fscr[bass.ds(g * FH, FH), :].partition_broadcast(P)).then_inc(f_bc, 16)
                for w, dst in ((0, qt), (1, kt_)):
                    for j in range(4):
                        if j == 3:
                            act.wait_ge(pe_blk, (q0 + w) * 4 + 4)
                            act.wait_ge(fy_t, g * 4)
                            for t in range(TT):
                                S.activation(dst[:, t, :], ps[4 * w + t][:, :], ACT.Copy).then_inc(ac, 1)
                                act.wait_ge(fss, g * 8 + 4 * w + t)
                                S.activation(sqb[:, :], ps[4 * w + t][:, :], ACT.Square).then_inc(fev, 1)
                        hi_ahead(q0 + w, j)
                for j in range(3):
                    hi_ahead(q0 + 2, j)
                act.wait_ge(pe_blk, q0 * 4 + 12)
                for t in range(TT):
                    S.activation(vt[:, t, :], ps[t][:, :], ACT.Copy).then_inc(fev, 1)
                hi_ahead(q0 + 2, 3)
                for j in range(4):
                    if j == 0:
                        for f in range(4):
                            act.wait_ge(f_tr, g * 8 + f + 1)
                            S.activation(qT[:, f, :], ps[4 + f][:, :], ACT.Copy, scale=qkw[:, 0:1]).then_inc(f_te, 1)
                    if j == 2:
                        for f in range(4):
                            act.wait_ge(f_tr, g * 8 + 4 + f + 1)
                            S.activation(kT[:, f, :], ps[4 + f][:, :], ACT.Copy,
                                         scale=par[:, C_KN:C_KN + 1]).then_inc(f_te, 1)
                    act.wait_ge(pe_blk, q0 * 4 + 12 + j + 1)
                    S.activation(gs[:, j, :], ps[j][:, :], ACT.Sigmoid).then_inc(fev, 1)
                    hi_ahead(q0 + 3, j)
                for u in range(UNITS):
                    a, i = divmod(u, TT)
                    n = P * (i + 1)
                    act.wait_ge(s_ns, g * UNITS + u + 1)
                    if u >= 2:
                        act.wait_ge(s_tr, g * UNITS + u - 1)
                    S.activation(kt_[:, u % 2, 0:n], scr[u % 2][:, 0:n], ACT.Exp, scale=-1.0,
                                 bias=small[:, u:u + 1], accum_out=ssq[:, u:u + 1]).then_inc(s_p, 1)
                for f in range(4):
                    act.wait_ge(fy_t, g * 4 + f + 1)
                    S.activation(tile(y1[0], g * 4 + f), scr[f % 2][:, :], ACT.Copy).then_inc(fy_hi, 1)
            residual(2, L + Q_OUT, 1, 3 * KT, False)
            norm(3, h3, 48 + SH2)
            mlp(1, a1, 3, h3, 4 * KT)

        @block.gpsimd
        def _(pool):
            G.memset(ident[:, :], 0.0).then_inc(gp, 1)
            G.memset(mhalf[:, :], -0.5).then_inc(gp, 1)
            G.memset(ones[:, :], 1.0)
            G.memset(meand[:, 0:1], 1.0 / D)
            G.memset(meand[:, 1:2], 1.0 / P)
            pool.wait_ge(gp, 1)
            G.affine_select(out=ident[:, :], in_=ident[:, :], compare_op=ALU.not_equal, fill=1.0,
                            base=0, pattern=[[-1, P]], channel_multiplier=1).then_inc(gp, 1)
            pool.wait_ge(gp, 3)
            G.tensor_copy(identb[:, :], ident[:, :]).then_inc(gp, 1)
            G.memset(causal[:, :], 0.0).then_inc(gp, 1)
            pool.wait_ge(gp, 5)
            G.affine_select(out=causal[:, :], in_=causal[:, :], compare_op=ALU.is_ge, fill=-3e38,
                            base=0, pattern=[[-1, P]], channel_multiplier=1).then_inc(gp, 1)
            n = 6
            for lv in range(MASKED):
                pool.wait_ge(gp, n)
                if lv:
                    m = 1 << (lv - 1)
                    nb = P // (2 * m)
                    v = sqb[:, 0:P].rearrange("p (b h m) -> p b h m", h=2, m=m)
                    G.memset(v[:, :, 0, :], 0.0)
                    G.memset(v[:, :, 1, :], 1.0).then_inc(gp, 1)
                    pool.wait_ge(gp, n + 1)
                    G.affine_select(out=v[:, :, 1, :], in_=v[:, :, 1, :], compare_op=ALU.is_ge, fill=0.0,
                                    base=0, pattern=[[-2 * m, nb], [0, m]], channel_multiplier=1).then_inc(gp, 1)
                    pool.wait_ge(gp, n + 2)
                    G.affine_select(out=v[:, :, 1, :], in_=v[:, :, 1, :], compare_op=ALU.is_gt, fill=0.0,
                                    base=m, pattern=[[2 * m, nb], [0, m]], channel_multiplier=-1).then_inc(gp, 1)
                    pool.wait_ge(gp, n + 3)
                    G.tensor_copy(masks[:, lv, :], sqb[:, 0:P]).then_inc(gp, 1)
                    n += 4
            pool.wait_ge(gp, n)
            G.memset(sqb[:, 0:1], 0.0).then_inc(consts, 1)

            def lo(quad_plus, j):
                pool.wait_ge(w_hi, quad_plus * 4 + j + 1)
                G.tensor_tensor(wlo[:, j, :], raw[:, j, :], whi[:, j, :].bitcast(F32), ALU.subtract).then_inc(w_lo, 1)

            def root(ready, ready_at, n, done, at=0):
                pool.wait_ge(ready, ready_at)
                G.tensor_tensor(rst[:, at:at + n], ssq[:, at:at + n], mhalf[:, 0:n], ALU.pow).then_inc(done, 1)

            for j in range(4):
                lo(0, j)
            root(n_var, 1, TT, n_rst)
            with pool.Fori(0, 2) as g:
                with pool.Fori(0, 3) as w:
                    for j in range(4):
                        lo(g * 4 + w + 1, j)
                for lv in range(1, SPLITS - 1):
                    m = 1 << (lv - 1)
                    for j in range(GH):
                        kv = hk[:, j, :].rearrange("p (b h m) -> p b h m", h=2, m=m)
                        tv = hf[:, j, :].rearrange("p (b h m) -> p b h m", h=2, m=m)
                        shape = [P, T // (2 * m), m]
                        pool.wait_ge(lvl, g * 40 + 4 * lv + j + 1)
                        G.tensor_tensor(kv[:, :, 0, :], kv[:, :, 0, :], tv[:, :, 1, 0:1].broadcast_to(shape),
                                        ALU.mult).then_inc(*((gp, 1) if lv < SPLITS - 2 else (kup, 1)))
                        if lv < SPLITS - 2:
                            pool.wait_ge(gp, g * 28 + n + 4 * (lv - 1) + j + 1)
                            pool.wait_ge(qup, g * 36 + 4 * lv + j + 1)
                            G.tensor_tensor(tv[:, :, 0, 0], tv[:, :, 0, 0], tv[:, :, 1, 0], ALU.mult).then_inc(kup, 1)
                    if lv % 2:
                        if lv // 2 < 4:
                            lo(g * 4 + 4, lv // 2)
                root(g_var, g + 1, 4 * GH, g_rst)
            with pool.Fori(Q_OUT + 1, Q_OUT + 3) as q:
                for j in range(4):
                    lo(q, j)
            root(n_var, 2, TT, n_rst)
            with pool.Fori(Q_MLP + 1, LAYER_QUADS + 1) as q:
                for j in range(4):
                    lo(q, j)
            root(n_var, 3, TT, n_rst)
            L = LAYER_QUADS
            with pool.Fori(0, 2) as g:
                for j in range(4):
                    lo(g * 4 + L + 1, j)
                root(f_var, g * 2 + 1, 32, f_rst)
                for j in range(4):
                    lo(g * 4 + L + 2, j)
                root(f_var, g * 2 + 2, 32, f_rst, 32)
                with pool.Fori(2, 4) as w:
                    for j in range(4):
                        lo(g * 4 + w + (L + 1), j)
            with pool.Fori(L + Q_OUT + 1, L + Q_OUT + 3) as q:
                for j in range(4):
                    lo(q, j)
            root(n_var, 4, TT, n_rst)
            with pool.Fori(L + Q_MLP + 1, QUADS) as q:
                for j in range(4):
                    lo(q, j)
            root(n_var, 5, TT, n_rst)

        @block.tensor
        def _(pe):
            def split(quad, j):
                pe.wait_ge(w_hi, quad * 4 + j + 1)
                pe.wait_ge(w_lo, quad * 4 + j + 1)

            def product(out, w, k, hh, first, last):
                wh, wl = whi[:, w, P * k:P * k + P], wlo[:, w, P * k:P * k + P]
                PE.matmul(out, wh, hh[0], start=first, stop=False)
                PE.matmul(out, wh, hh[1], start=False, stop=False)
                return PE.matmul(out, wl, hh[0], start=False, stop=last)

            def feature_block(quad, j, bank, h, k0=0, first=True, last=True, ready=None):
                split(quad, j)
                for k in range(KT):
                    if ready is not None:
                        pe.wait_ge(h_lo, ready + k + 1)
                    mm = product(ps[bank][:, :], j, k, [h[0][:, k0 + k, :], h[1][:, k0 + k, :]],
                                 first and k == 0, last and k == KT - 1)
                mm.then_inc(pe_blk, 1)

            def token_blocks(quad, bank, h, ready=None):
                for j in range(4):
                    split(quad, j)
                    for kk in range(2):
                        k = 2 * j + kk
                        if ready is not None:
                            pe.wait_ge(h_lo, ready + k + 1)
                        for t in range(TT):
                            o = ps[bank + t][:, :]
                            hh, hl = cols(h[0][:, k, :], t), cols(h[1][:, k, :], t)
                            w0 = slice(T * kk, T * kk + T)
                            PE.matmul(o, hh, whi[:, j, w0], start=k == 0, stop=False)
                            PE.matmul(o, hl, whi[:, j, w0], start=False, stop=False)
                            mm = PE.matmul(o, hh, wlo[:, j, w0], start=False, stop=k == KT - 1)
                    mm.then_inc(pe_blk, 1)

            def norm(n):
                pe.wait_ge(x_acc, KT * NORM_SQ[n])
                for t in range(TT):
                    mm = PE.matmul(ps[6][:, t:t + 1], cols(acc, t), meand[:, 0:1], start=True, stop=True)
                mm.then_inc(n_sum, 1)
                pe.wait_ge(n_dg, n + 1)
                for t in range(TT):
                    mm = PE.matmul(cols(ps[7], t), ones[:, :], cols(sqb, t), start=True, stop=True)
                mm.then_inc(n_bc, 1)

            pe.wait_ge(consts, 1)
            norm(0)
            with pe.Fori(0, 2) as g:
                q0 = g * 4
                pe.wait_ge(y_t, g * 4)
                for j in range(4):
                    feature_block(q0, j, j, h0, ready=0 if j == 0 else None)
                for j in range(4):
                    feature_block(q0 + 1, j, 4 + j, h0)
                pe.wait_ge(ev, g * 16 + 4)
                token_blocks(q0 + 2, 0, h0)
                for lv in range(SPLITS):
                    for j in range(GH):
                        if lv == 0:
                            pe.wait_ge(kf, g * 4 + j + 1)
                            if j == 0:
                                pe.wait_ge(ev, g * 16 + 12)
                        else:
                            pe.wait_ge(qup, g * 36 + 4 * (lv - 1) + j + 1)
                            if lv >= 2:
                                pe.wait_ge(kup, g * 32 + 4 * (lv - 2) + j + 1)
                            if lv <= MASKED:
                                pe.wait_ge(sel, g * 32 + 4 * (lv - 1) + j + 1)
                        kk, qq = hk[:, j, :], hq[:, j, :]
                        if lv < MASKED:
                            for t in range(TT):
                                mm = PE.matmul(cols(ps[j], t), cols(kk, t), cols(qq, t), start=True, stop=True)
                        elif lv == 8:
                            if j == 0:
                                pe.wait_ge(ev, g * 16 + 8)
                            PE.matmul(cols(ps[j], 0), cols(kk, 0), cols(qq, 1), start=True, stop=True)
                            mm = PE.matmul(cols(ps[j], 3), cols(kk, 2), cols(qq, 3), start=True, stop=True)
                        else:
                            y = ps[6 + j // 2][:, 256 * (j % 2):256 * (j % 2) + 256]
                            PE.matmul(ps[j][:, 128:384], cols(kk, 0), qq[:, 256:512], start=True, stop=True)
                            mm = PE.matmul(y, cols(kk, 1), qq[:, 256:512], start=True, stop=True)
                        mm.then_inc(lvl, 1)
                    if lv in (1, 3, 5, 7):
                        j = lv // 2
                        pe.wait_ge(ev, g * 16 + (8 if j < 2 else 12 + j - 1))
                        feature_block(q0 + 3, j, 4 + j % 2, h0)

                def summed(j):
                    pe.wait_ge(o_ev, g * 4 + j + 1)
                    for t in range(TT):
                        mm = PE.matmul(ps[6][:, 4 * j + t:4 * j + t + 1], cols(hk[:, j, :], t), meand[:, 1:2],
                                       start=True, stop=True)
                    if j == GH - 1:
                        mm.then_inc(g_sum, 1)

                for j in range(GH):
                    pe.wait_ge(off, g * 4 + j + 1)
                    if j < 2:
                        pe.wait_ge(ev, g * 16 + 16)
                    else:
                        pe.wait_ge(o_ev, g * 4 + j - 1)
                    o = ps[4 + j % 2]
                    v = [hv[:, s, P * j:P * j + P] for s in range(TT)]
                    PE.matmul(cols(o, 0), v[0], cols(adiag[:, j, :], 0), start=True, stop=False, skip_group_check=True)
                    PE.matmul(o[:, 128:512], v[0], hf[:, j, 0:384], start=False, stop=False, skip_group_check=True)
                    PE.matmul(o[:, 256:512], v[1], hk[:, j, 256:512], start=False, stop=False, skip_group_check=True)
                    PE.matmul(o[:, 384:512], v[2], hf[:, j, 384:512], start=False, stop=False, skip_group_check=True)
                    for s in range(1, TT):
                        mm = PE.matmul(cols(o, s), v[s], cols(adiag[:, j, :], s), start=False, stop=s == TT - 1,
                                       skip_group_check=True)
                    mm.then_inc(o_pe, 1)
                    if j >= 1:
                        if j == 1:
                            pe.wait_ge(off, g * 4 + 2)
                        summed(j - 1)
                summed(GH - 1)
                for j in range(GH):
                    pe.wait_ge(g_dg, g * 4 + j + 1)
                    for t in range(TT):
                        mm = PE.matmul(cols(ps[j], t), ones[:, :], cols(DG[j % 2], t), start=True, stop=True)
                    mm.then_inc(g_bc, 1)

            def w_out(quad, y, y_done, upd0):
                pe.wait_ge(*y_done)
                with pe.Fori(0, 2) as q:
                    for j in range(4):
                        pe.wait_ge(x_upd, q * 4 + (upd0 + j - 3)) if upd0 + j - 3 > 0 else (
                            pe.wait_ge(x_upd, q * 4))
                        feature_block(q + quad, j, j, y)

            def mlp(layer, h, a, n):
                base = layer * LAYER_QUADS + Q_MLP
                for half in range(2):
                    with pe.Fori(0, 4) as q:
                        for j in range(4):
                            pe.wait_ge(ff_r, q * 4 + (32 * layer + 16 * half + j - 3 if layer or half or j == 3 else 0))
                            feature_block(q + base + 8 * half, j, j, h, ready=KT * n if j == 0 else None)
                    with pe.Fori(0, 4) as q:
                        for j in range(4):
                            if j % 2 == 0:
                                pe.wait_ge(x_upd, q * 2 + (UPD[2 * layer + 1] + KT * half + j // 2 - 1))
                            if j == 0:
                                pe.wait_ge(ff_lo, 32 * layer + 16 * (half + 1))
                            feature_block(q + base + 8 * half + 4, j, 4 + j // 2, a, k0=KT * (j % 2),
                                          first=j % 2 == 0, last=j % 2 == 1)

            w_out(Q_OUT, y0, (y_lo, 8), 0)
            norm(1)
            mlp(0, h1, a0, 1)
            norm(2)
            pe.wait_ge(f_wl, 1)
            for k in range(KT):
                pe.wait_ge(h_lo, 2 * KT + k + 1)
                wh, wl = cols(wfs[0], k), cols(wfs[1], k)
                PE.matmul(ps[0][:, :], wh, h2[0][:, k, :], start=k == 0, stop=False)
                PE.matmul(ps[0][:, :], wh, h2[1][:, k, :], start=False, stop=False)
                mm = PE.matmul(ps[0][:, :], wl, h2[0][:, k, :], start=False, stop=k == KT - 1)
            mm.then_inc(f_pe, 1)
            L = LAYER_QUADS
            pe.wait_ge(f_out, 1)
            with pe.Fori(0, 2) as g:
                q0 = g * 4 + L
                pe.wait_ge(fy_t, g * 4)
                token_blocks(q0, 0, h2)
                token_blocks(q0 + 1, 4, h2)
                pe.wait_ge(fev, g * 16 + 4)
                token_blocks(q0 + 2, 0, h2)

                def turn(w, src):
                    pe.wait_ge(f_nrm, g * 8 + 4 * w + 4)
                    pe.wait_ge(fev, g * 16 + 8)
                    if w:
                        pe.wait_ge(f_te, g * 8 + 4)
                    for f in range(4):
                        for t in range(TT):
                            mm = PE.transpose(cols(ps[4 + f], t), cols(src[:, t, :], f), ident[:, :])
                        mm.then_inc(f_tr, 1)

                turn(0, qt)
                for j in range(4):
                    if j == 2:
                        turn(1, kt_)
                    pe.wait_ge(fev, g * 16 + 8 + j + 1)
                    feature_block(q0 + 3, j, j, h2)

                def scores(u):
                    a, i = divmod(u, TT)
                    r, f = 64 * (a % 2), a // 2
                    if u >= 2:
                        pe.wait_ge(s_ns, g * UNITS + u - 1)
                    n = P * (i + 1)
                    PE.matmul(ps[u % 2][:, 0:n], qT[r:r + 64, f, P * i:P * i + P], kT[r:r + 64, f, 0:n],
                              start=True, stop=False, skip_group_check=True)
                    PE.matmul(ps[u % 2][:, n - P:n], identb[:, :], causal[:, :],
                              start=False, stop=True, skip_group_check=True).then_inc(s_pe, 1)

                def transposes(u):
                    i = u % TT
                    pe.wait_ge(s_p, g * UNITS + u + 1)
                    if u >= 2:
                        pe.wait_ge(s_pt, g * UNITS + u - 1)
                    for s in range(i + 1):
                        mm = PE.transpose(cols(ps[2 + u % 2], s), cols(kt_[:, u % 2, :], s), ident[:, :])
                    mm.then_inc(s_tr, 1)

                def values(u):
                    a, i = divmod(u, TT)
                    pe.wait_ge(s_pt, g * UNITS + u + 1)
                    if i == 0 and a >= 2:
                        pe.wait_ge(s_o, g * FH + a - 1)
                    for s in range(i + 1):
                        mm = PE.matmul(ps[4 + a % 2][:, DH * i:DH * i + DH], cols(pT[:, u % 2, :], s),
                                       vt[:, s, DH * a:DH * a + DH], start=s == 0, stop=s == i)
                    mm.then_inc(s_pv, 1)

                pe.wait_ge(fev, g * 16 + 16)
                pe.wait_ge(f_te, g * 8 + 8)
                scores(0)
                for u in range(UNITS):
                    if u + 1 < UNITS:
                        scores(u + 1)
                    transposes(u)
                    if u >= 1:
                        values(u - 1)
                values(UNITS - 1)
                pe.wait_ge(s_o, g * FH + FH)
                for f in range(4):
                    for t in range(TT):
                        mm = PE.transpose(cols(ps[4 + f], t), cols(qt[:, t, :], f), ident[:, :])
                    mm.then_inc(ot_tr, 1)
            w_out(L + Q_OUT, y1, (fy_lo, 8), UPD[2])
            norm(3)
            mlp(1, h3, a1, 3)
            norm(4)

        @block.vector
        def _(dve):
            chain = [0]

            def link(ins):
                chain[0] += 1
                ins.then_inc(dv, 1)
                dve.wait_ge(dv, chain[0])

            def eps_var(bank_cols, n, at=0):
                return V.tensor_scalar(ssq[:, at:at + n], bank_cols, EPS, None, ALU.add)

            def diagonals(dst, roots):
                return V.tensor_tensor(dst.rearrange("p (t q) -> p t q", q=P),
                                       ident[:, :].unsqueeze(1).broadcast_to([P, TT, P]),
                                       roots.unsqueeze(2).broadcast_to([P, TT, P]), ALU.mult)

            def root_of_x(n):
                dve.wait_ge(n_sum, n + 1)
                eps_var(ps[6][:, 0:TT], TT).then_inc(n_var, 1)
                dve.wait_ge(n_rst, n + 1)
                diagonals(sqb[:, :], rst[:, 0:TT]).then_inc(n_dg, 1)
                dve.wait_ge(n_bc, n + 1)

            def norm(n, h, gain0, shift):
                root_of_x(n)

                def t_of(k):
                    if k >= 2:
                        dve.wait_ge(h_lo, n * KT + k - 1)
                    V.scalar_tensor_tensor(out=scr[k % 2][:, :], in0=x[:, k, :], scalar=gain[:, gain0 + k:gain0 + k + 1],
                                           in1=ps[7][:, :], op0=ALU.mult, op1=ALU.mult).then_inc(h_t, 1)

                t_of(0)
                for k in range(KT):
                    if k + 1 < KT:
                        t_of(k + 1)
                    dve.wait_ge(h_hi, n * KT + k + 1)
                    V.scalar_tensor_tensor(out=h[1][:, k, :], in0=scr[k % 2][:, :],
                                           scalar=mod[:, shift + k:shift + k + 1],
                                           in1=h[0][:, k, :].bitcast(F32), op0=ALU.add,
                                           op1=ALU.subtract).then_inc(h_lo, 1)

            def modulation(mq, j):
                s = j % 2
                dve.wait_ge(mod_in[s], mq * 32 + 16 * (j // 2 + 1))
                if j == 0:
                    dve.wait_ge(mod_set, mq)
                V.tensor_tensor_reduce(out=mring[:, s, :], in0=mring[:, s, :], in1=cb[:, :], scale=1.0, scalar=0.0,
                                       op0=ALU.mult, op1=ALU.add, accum_out=dots[:, j:j + 1]).then_inc(mod_used, 1)
                if j == 3:
                    dve.wait_ge(mod_used, mq * 4 + 4)
                    V.tensor_copy(mod[:, bass.ds(mq * 4 + 16, 4)], dots[:, :]).then_inc(mod_set, 1)

            def add_bias(lo_, hi_):
                link(V.tensor_tensor(mod[:, lo_:hi_], mod[:, lo_:hi_], par[:, C_BMOD + lo_:C_BMOD + hi_], ALU.add))

            def gains(i, norm_col, scale_col):
                link(V.scalar_tensor_tensor(out=gain[:, KT * i:KT * i + KT], in0=mod[:, scale_col:scale_col + KT],
                                            scalar=1.0, in1=par[:, norm_col:norm_col + KT],
                                            op0=ALU.add, op1=ALU.mult))

            def half_y(base, j, hi_sem, lo_sem, y):
                dve.wait_ge(hi_sem, base + (j + 1))
                V.tensor_tensor(tile(y[1], base + j), scr[j % 2][:, :], tile(y[0], base + j).bitcast(F32),
                                ALU.subtract).then_inc(lo_sem, 1)

            dve.wait_ge(par_in, 16)
            lb = [par[:, C_LB + KT * i:C_LB + KT * i + KT] for i in range(3)]
            link(V.tensor_tensor(small[:, 0:8], lb[0], lb[1], ALU.max))
            link(V.tensor_tensor(small[:, 8:16], small[:, 0:8], lb[2], ALU.max))
            for i in range(3):
                ins = V.tensor_tensor(lbc[:, KT * i:KT * i + KT], lb[i], small[:, 8:16], ALU.subtract)
            ins.then_inc(lb_mx, 1)
            V.tensor_scalar(qkw[:, :], par[:, C_QN:C_QN + 1], DH ** -0.5, None, ALU.mult)
            dve.wait_ge(lb_ex, 1)
            link(V.tensor_tensor(small[:, 0:8], lbc[:, 32:40], lbc[:, 40:48], ALU.add))
            link(V.tensor_tensor(small[:, 8:16], small[:, 0:8], lbc[:, 24:32], ALU.add))
            link(V.reciprocal(small[:, 16:24], small[:, 8:16]))
            V.tensor_tensor(lbc[:, 0:8], lbc[:, 24:32], small[:, 16:24], ALU.mult)
            link(V.tensor_tensor(lbc[:, 8:16], small[:, 0:8], small[:, 16:24], ALU.mult))

            dve.wait_ge(cact, 1)
            for m in range(16):
                if m % 4 == 0:
                    dve.wait_ge(modf_in[m // 4], 16)
                ins = V.tensor_tensor_reduce(out=modf[:, m, :], in0=modf[:, m, :], in1=cb[:, :], scale=1.0, scalar=0.0,
                                             op0=ALU.mult, op1=ALU.add, accum_out=mod[:, m:m + 1])
            link(ins)
            add_bias(0, 16)
            gains(0, C_N1, SC1)
            dve.wait_ge(consts, 1)
            link(V.memset(acc[:, :], 0.0))
            for k in range(KT):
                dve.wait_ge(x_sq, k + 1)
                if k:
                    dve.wait_ge(x_acc, k)
                V.tensor_tensor(acc[:, :], acc[:, :], sqb[:, :], ALU.add).then_inc(x_acc, 1)
            norm(0, h0, 0, SH1)

            with dve.Fori(0, 2) as g:
                for j in range(4):
                    modulation(g * 4, j)
                for j in range(4):
                    dve.wait_ge(ev, g * 16 + 4 + j + 1)
                    V.tensor_scalar(hf[:, j, :], hf[:, j, :], col(lbc, g * 4 + (8 + j)), col(lbc, g * 4 + j),
                                    ALU.mult, ALU.add)
                    V.tensor_scalar(hk[:, j, :], hk[:, j, :], col(lbc, g * 4 + (8 + j)), None, ALU.mult).then_inc(kf, 1)
                    modulation(g * 4 + 1, j)
                for j in range(4):
                    modulation(g * 4 + 2, j)
                for lv in range(SPLITS - 1):
                    m = 1 << max(lv - 1, 0)
                    for j in range(GH):
                        dve.wait_ge(lvl, g * 40 + 4 * lv + j + 1)
                        bank = ps[j][:, :].rearrange("p (t q) -> p t q", q=P)
                        ad = adiag[:, j, :].rearrange("p (t q) -> p t q", q=P)
                        if lv == 0:
                            V.tensor_tensor(hq[:, j, :], hq[:, j, :], hf[:, j, :], ALU.mult).then_inc(qup, 1)
                            V.tensor_tensor(ad, bank, ident[:, :].unsqueeze(1).broadcast_to([P, TT, P]),
                                            ALU.mult).then_inc(sel, 1)
                            continue
                        qv = hq[:, j, :].rearrange("p (b h m) -> p b h m", h=2, m=m)
                        tv = hf[:, j, :].rearrange("p (b h m) -> p b h m", h=2, m=m)
                        V.tensor_tensor(qv[:, :, 1, :], qv[:, :, 1, :],
                                        tv[:, :, 0, 0:1].broadcast_to([P, T // (2 * m), m]), ALU.mult).then_inc(qup, 1)
                        if lv < MASKED:
                            V.copy_predicated(ad, masks[:, lv, :].unsqueeze(1).broadcast_to([P, TT, P]),
                                              bank).then_inc(sel, 1)
                    if lv in (1, 3, 5, 7):
                        j = lv // 2
                        modulation(g * 4 + 3, j)
                for j in range(GH):
                    dve.wait_ge(o_ev, g * 4 + j + 1)
                    ins = V.tensor_tensor(hg_[:, j, :], hg_[:, j, :], hq[:, j, :], ALU.mult)
                ins.then_inc(dv, 1)
                dve.wait_ge(g_sum, g + 1)
                eps_var(ps[6][:, 0:16], 16).then_inc(g_var, 1)
                dve.wait_ge(g_rst, g + 1)
                dve.wait_ge(dv, g + (chain[0] + 1))

                def diag(j):
                    diagonals(DG[j % 2][:, :], rst[:, 4 * j:4 * j + 4]).then_inc(g_dg, 1)

                diag(0)
                diag(1)
                for j in range(GH):
                    dve.wait_ge(g_bc, g * 4 + j + 1)
                    if j >= 2:
                        dve.wait_ge(y_lo, g * 4 + j - 1)
                    V.scalar_tensor_tensor(out=scr[j % 2][:, :], in0=hg_[:, j, :], scalar=par[:, C_GN:C_GN + 1],
                                           in1=ps[j][:, :], op0=ALU.mult, op1=ALU.mult).then_inc(y_t, 1)
                    if j + 2 < GH:
                        diag(j + 2)
                    if j >= 1:
                        half_y(g * 4, j - 1, y_hi, y_lo, y0)
                half_y(g * 4, GH - 1, y_hi, y_lo, y0)
            chain[0] += 2

            def residual(quads, q0, per, gate, upd0, start_at):
                link(V.memset(acc[:, :], 0.0))
                def add(n, base):
                    dve.wait_ge(x_sq, n + (base + 1))
                    dve.wait_ge(x_acc, n + base)
                    V.tensor_tensor(acc[:, :], acc[:, :], sqb[:, :], ALU.add).then_inc(x_acc, 1)
                with dve.Fori(0, quads) as q:
                    for j in range(0, 4, per):
                        n = q * (4 // per) + j // per
                        bank = j if per == 1 else 4 + j // 2
                        dve.wait_ge(pe_blk, (q + q0) * 4 + j + per)
                        V.scalar_tensor_tensor(out=tile(x, n), in0=ps[bank][:, :], scalar=col(mod, n + gate),
                                               in1=tile(x, n), op0=ALU.mult, op1=ALU.add).then_inc(x_upd, 1)
                        if per == 2 and start_at is not None:
                            for s in range(2):
                                modulation(q + start_at, j + s)
                        add(n, upd0 + KT)

            def mlp(layer, a, gate, upd0):
                base = layer * LAYER_QUADS + Q_MLP
                for half in range(2):
                    with dve.Fori(0, 4) as q:
                        for j in range(4):
                            n = q * 4 + (32 * layer + 16 * half + j)
                            dve.wait_ge(ff_r, n + 1)
                            V.tensor_tensor(scr[j % 2][:, :], scr[j % 2][:, :], scr[j % 2][:, :], ALU.mult).then_inc(ff_sq, 1)
                            if layer == 0:
                                modulation(q + 8 + 8 * half, j)
                            dve.wait_ge(ff_hi, n + 1)
                            V.tensor_tensor(tile(a[1], q * 4 + j), scr[j % 2][:, :], tile(a[0], q * 4 + j).bitcast(F32),
                                            ALU.subtract).then_inc(ff_lo, 1)
                    residual(4, base + 8 * half + 4, 2, gate, upd0 + KT * half,
                             12 if layer == 0 and half == 0 else None)

            dve.wait_ge(mod_set, 8)
            add_bias(16, 48)
            gains(1, C_N2, SC2)
            residual(2, Q_OUT, 1, G1, 0, None)
            norm(1, h1, KT, SH2)
            mlp(0, a0, G2, KT)
            dve.wait_ge(mod_set, 20)
            add_bias(48, 96)
            gains(2, C_N1 + 8, 48 + SC1)
            gains(3, C_N2 + 8, 48 + SC2)
            dve.wait_ge(f_w, 1)
            V.tensor_tensor(wfs[1][:, :], wf[:, :], wfs[0][:, :].bitcast(F32), ALU.subtract).then_inc(f_wl, 1)
            norm(2, h2, 2 * KT, 48 + SH1)
            dve.wait_ge(f_pe, 1)
            link(V.memset(acc[:, :], 1.0))
            dve.wait_ge(ac, 1)
            link(V.tensor_scalar(scr[0][:, :], ps[0][:, :], par[:, C_BF:C_BF + 1], 0.0, ALU.add, ALU.min))
            dve.wait_ge(f_ln, 1)
            link(V.tensor_tensor(scr[1][:, :], sqb[:, :], scr[0][:, :], ALU.subtract))
            V.tensor_tensor_scan(out=acc[:, :], data0=acc[:, :], data1=scr[1][:, :], initial=0.0,
                                 op0=ALU.mult, op1=ALU.add).then_inc(f_out, 1)
            with dve.Fori(0, 2) as g:
                for w, dst in ((0, qt), (1, kt_)):
                    for t in range(TT):
                        dve.wait_ge(fev, g * 16 + 4 * w + t + 1)
                        V.tensor_reduce(out=ssq[:, 32 * w + 8 * t:32 * w + 8 * t + 8],
                                        in_=sqb[:, :].rearrange("p (a d) -> p a d", d=DH), axis=AX.X,
                                        op=ALU.add).then_inc(fss, 1)
                    dve.wait_ge(fss, g * 8 + 4 * w + 4)
                    V.tensor_scalar(ssq[:, 32 * w:32 * w + 32], ssq[:, 32 * w:32 * w + 32], 1.0 / DH, EPS,
                                    ALU.mult, ALU.add).then_inc(f_var, 1)
                for w, dst in ((0, qt), (1, kt_)):
                    dve.wait_ge(f_rst, g * 2 + w + 1)
                    for t in range(TT):
                        V.tensor_tensor(dst[:, t, :].rearrange("p (a d) -> p a d", d=DH),
                                        dst[:, t, :].rearrange("p (a d) -> p a d", d=DH),
                                        rst[:, 32 * w + 8 * t:32 * w + 8 * t + 8].unsqueeze(2).broadcast_to([P, 8, DH]),
                                        ALU.mult).then_inc(f_nrm, 1)
                dve.wait_ge(f_bc, g * 16 + 16)

                def biased(u):
                    a, i = divmod(u, TT)
                    n = P * (i + 1)
                    V.tensor_tensor_reduce(out=scr[u % 2][:, 0:n], in0=ps[u % 2][:, 0:n], in1=fb[:, a, 0:n],
                                           scale=-1.0, scalar=3e38, op0=ALU.add, op1=ALU.min,
                                           accum_out=small[:, u:u + 1]).then_inc(s_ns, 1)

                def scored(u):
                    dve.wait_ge(s_pe, g * UNITS + u + 1)
                    if u >= 2:
                        dve.wait_ge(s_p, g * UNITS + u - 1)

                def turned(u):
                    n = P * (u % TT + 1)
                    dve.wait_ge(s_tr, g * UNITS + u + 1)
                    if u + 1 < UNITS:
                        scored(u + 1)
                    if u >= 2:
                        dve.wait_ge(s_pv, g * UNITS + u - 1)
                    V.tensor_copy(pT[:, u % 2, 0:n], ps[2 + u % 2][:, 0:n]).then_inc(s_pt, 1)

                def head_out(a):
                    dve.wait_ge(s_pv, g * UNITS + TT * a + TT)
                    V.reciprocal(rst[:, 4 * a:4 * a + 4], ssq[:, 4 * a:4 * a + 4]).then_inc(dv, 1)
                    dve.wait_ge(dv, g * FH + (chain[0] + a + 1))
                    V.tensor_tensor(qt[:, :, DH * a:DH * a + DH],
                                    ps[4 + a % 2][:, 0:TT * DH].rearrange("p (t d) -> p t d", d=DH),
                                    rst[:, 4 * a:4 * a + 4].unsqueeze(2).broadcast_to([P, TT, DH]),
                                    ALU.mult).then_inc(s_o, 1)

                scored(0)
                V.memset(dots[:, 0:1], 0.0)
                biased(0)
                for u in range(UNITS):
                    turned(u)
                    if u + 1 < UNITS:
                        biased(u + 1)
                    if u % TT == 1 and u > TT:
                        head_out(u // TT - 1)
                head_out(FH - 1)
                for f in range(4):
                    dve.wait_ge(ot_tr, g * 4 + f + 1)
                    if f >= 2:
                        dve.wait_ge(fy_lo, g * 4 + f - 1)
                    V.tensor_tensor(scr[f % 2][:, :], ps[4 + f][:, :], gs[:, f, :], ALU.mult).then_inc(fy_t, 1)
                    if f >= 1:
                        half_y(g * 4, f - 1, fy_hi, fy_lo, y1)
                half_y(g * 4, 3, fy_hi, fy_lo, y1)
            chain[0] += 2 * FH
            residual(2, LAYER_QUADS + Q_OUT, 1, 48 + G1, 3 * KT, None)
            norm(3, h3, 3 * KT, 48 + SH2)
            mlp(1, a1, 48 + G2, 4 * KT)
            root_of_x(4)
            for k in range(KT):
                V.scalar_tensor_tensor(out=x[:, k, :], in0=x[:, k, :], scalar=par[:, C_FIN + k:C_FIN + k + 1],
                                       in1=ps[7][:, :], op0=ALU.mult, op1=ALU.mult).then_inc(out_t_ready, 1)


_INS = ("x_t", "c_row", "stream", "mod_rows", "w_forget", "params")


def _laid_out(i):
    def feature_block(w, n):
        return w[:, P * n:P * n + P].reshape(KT, P, P).transpose(1, 0, 2).reshape(P, D)

    def token_blocks(w, c0):
        part = w[:, c0:c0 + T].reshape(4, 2, P, T).transpose(0, 2, 1, 3)
        return list(part.reshape(4, P, D))

    hg_in, fox_in = i["hg_w_in"][0], i["fox_w_in"][0]
    blocks = []
    for layer in range(2):
        for g in range(2):
            if layer == 0:
                for part in (0, 1):
                    blocks += [feature_block(hg_in, 8 * part + 4 * g + j) for j in range(4)]
                blocks += token_blocks(hg_in, 2 * D + T * g)
                blocks += [feature_block(hg_in, 24 + 4 * g + j) for j in range(4)]
            else:
                for part in range(3):
                    blocks += token_blocks(fox_in, D * part + T * g)
                blocks += [feature_block(fox_in, 24 + 4 * g + j) for j in range(4)]
        w_out = i["hg_w_out" if layer == 0 else "fox_w_out"][0]
        blocks += [feature_block(w_out, n) for n in range(KT)]
        w1, w2 = i["mlp_w1"][layer], i["mlp_w2"][layer]
        for half in range(2):
            blocks += [feature_block(w1, HALF * half + n) for n in range(HALF)]
            for n in range(KT):
                for s in range(2):
                    k0 = D * (2 * half + s)
                    blocks.append(feature_block(w2[k0:k0 + D], n))
    stream = np.stack(blocks)
    mod_rows = np.ascontiguousarray(i["w_mod"].transpose(0, 2, 1)).reshape(2 * 48, P, D)
    gate = np.zeros((D, P), np.float32)
    gate[:, 0:HEADS] = fox_in[:, 4 * D:]

    def columns(v):
        return v.reshape(-1, P).T

    bias = np.zeros((P, 1), np.float32)
    bias[0:HEADS, 0] = i["fox_b_f"][0]
    twice = [np.concatenate([i[n][0], i[n][0]])[:, None] for n in ("fox_qn_w", "fox_kn_w")]
    params = np.concatenate(
        [columns(i["norm1_w"].reshape(-1)), columns(i["norm2_w"].reshape(-1)), columns(i["final_w"]),
         columns(i["hg_lb"].reshape(-1)), i["hg_gn_w"][0][:, None], *twice, bias,
         columns(i["b_mod"].reshape(-1))], axis=1)
    x_t = np.ascontiguousarray(i["x"][0].T).reshape(KT, P, T).transpose(1, 0, 2)
    return {"x_t": x_t, "c_row": i["c"], "stream": stream, "mod_rows": mod_rows,
            "w_forget": feature_block(gate, 0), "params": params}


def kernel(**inputs):
    import concourse.bacc as bacc
    from concourse.bass_utils import run_bass_kernel_spmd

    laid = _laid_out({n: np.asarray(a) for n, a in inputs.items()})
    nc = bacc.Bacc("TRN2", target_bir_lowering=False, num_devices=1)
    arrays, args = {}, []
    for name in _INS:
        arrays[name] = np.ascontiguousarray(laid[name])
        args.append(nc.dram_tensor(name, arrays[name].shape, F32, kind="ExternalInput").ap())
    args.append(nc.dram_tensor("out_t", (P, KT, T), F32, kind="ExternalOutput").ap())
    build(nc, *args)
    r = run_bass_kernel_spmd(nc, [arrays], core_ids=[0])
    got = np.asarray(r.results[0]["out_t"])
    return np.ascontiguousarray(got.transpose(2, 1, 0).reshape(1, T, D))
```

```python
import numpy as np
import concourse.bass as bass
import concourse.mybir as mybir
from concourse.alu_op_type import AluOpType as ALU
from contextlib import ExitStack

F32 = mybir.dt.float32
F32R = mybir.dt.float32r
BF16 = mybir.dt.bfloat16
U8 = mybir.dt.uint8
ACT = mybir.ActivationFunctionType
AX = mybir.AxisListType

P = 128
T = 512
TT = T // P
D = 1024
KT = D // P
EPS = 1e-6
HEADS = 16
DH = 64
GROUPS = 4
GH = 2
FH = 4
GW = D // GROUPS
FF = 4 * D
HALF = FF // 2 // P

Q_IN, Q_OUT, Q_MLP = 0, 8, 10
LAYER_QUADS = 26
QUADS = 2 * LAYER_QUADS

C_N1, C_N2, C_FIN, C_LB, C_GN, C_QN, C_KN, C_BF, C_BMOD = 0, 16, 32, 40, 64, 65, 66, 67, 68
C_ALL = C_BMOD + 96
SH1, SC1, G1, SH2, SC2, G2 = (8 * i for i in range(6))

MASKED = 8
SPLITS = 10


def build(nc, x_t, c_row, stream, mod_rows, w_forget, params, out_t):
    keep = ExitStack()
    with keep:
        def sem(name):
            return keep.enter_context(nc.semaphore(name))

        def sb(name, shape, dt, ctx=keep):
            return ctx.enter_context(nc.sbuf_tensor(name, shape, dt))

        x = sb("x", [P, KT, T], F32)
        raw = sb("raw", [P, 4, D], F32)
        whi = sb("whi", [P, 4, D], F32R)
        wlo = sb("wlo", [P, 4, D], F32R)
        par = sb("par", [P, C_ALL], F32)
        mod = sb("mod", [P, 96], F32)
        gain = sb("gain", [P, 4 * KT], F32)
        small = sb("small", [P, 64], F32)
        dots = sb("dots", [P, 4], F32)
        qkw = sb("qkw", [P, 1], F32)
        ident = sb("ident", [P, P], F32)
        identb = sb("identb", [P, P], BF16)
        causal = sb("causal", [P, P], BF16)
        ones = sb("ones", [P, P], F32)
        mhalf = sb("mhalf", [P, 32], F32)
        ssq = sb("ssq", [P, 64], F32)
        rst = sb("rst", [P, 64], F32)
        den = sb("den", [P, 64], F32)
        meand = sb("meand", [P, 2], F32)
        scr = [sb(f"scr{i}", [P, T], F32) for i in range(2)]
        sqb = sb("sqb", [P, T], F32)
        acc = sb("acc", [P, T], F32)

        layer0 = ExitStack()
        mring = sb("mring", [P, 2, D], F32, layer0)
        cb = sb("cb", [P, D], F32, layer0)
        masks = sb("masks", [P, MASKED, P], U8, layer0)
        lbc = sb("lbc", [P, 6 * KT], F32, layer0)

        head0 = ExitStack()
        modf = sb("modf", [P, 16, D], F32, head0)
        head0.close()
        hg = ExitStack()
        hq, hk, hf = (sb(n, [P, 2 * GH, T], F32, hg) for n in ("hq", "hk", "hf"))
        hv = sb("hv", [P, TT, T], F32, hg)
        hgate = sb("hgate", [P, GH, T], F32, hg)
        adiag = sb("adiag", [P, GH, T], F32, hg)
        h0 = [sb(n, [P, KT, T], F32R, hg) for n in ("h0hi", "h0lo")]
        y0 = [sb(n, [P, KT, T], F32R, hg) for n in ("y0hi", "y0lo")]
        hg.close()
        mlp0 = ExitStack()
        a0 = [sb(n, [P, HALF, T], F32R, mlp0) for n in ("a0hi", "a0lo")]
        h1 = [sb(n, [P, KT, T], F32R, mlp0) for n in ("h1hi", "h1lo")]
        wf = sb("wf", [P, D], F32, mlp0)
        wfs = [sb(n, [P, D], F32R, mlp0) for n in ("wfhi", "wflo")]
        mlp0.close()
        layer0.close()
        fox = ExitStack()
        qkt = [sb(n, [P, TT, GW], F32, fox) for n in ("qt", "kt")]
        qkT = [sb(n, [P, 4, T], F32, fox) for n in ("qT", "kT")]
        vt = sb("vt", [P, TT, 2 * GW], F32, fox)
        gs = sb("gs", [P, 2, T], F32, fox)
        ot = sb("ot", [P, TT, GW], F32, fox)
        prob = sb("prob", [P, 2, T], F32, fox)
        pT = sb("pT", [P, 2, T], F32, fox)
        fb = sb("fb", [P, 2 * FH, T], F32, fox)
        h2 = [sb(n, [P, KT, T], F32R, fox) for n in ("h2hi", "h2lo")]
        y1 = [sb(n, [P, KT, T], F32R, fox) for n in ("y1hi", "y1lo")]
        fox.close()
        mlp1 = ExitStack()
        a1 = [sb(n, [P, HALF, T], F32R, mlp1) for n in ("a1hi", "a1lo")]
        h3 = [sb(n, [P, KT, T], F32R, mlp1) for n in ("h3hi", "h3lo")]
        mlp1.close()
        fscr = nc.dram_tensor("negf", [HEADS, T], F32).ap()

        ps = [keep.enter_context(nc.psum_tensor(f"bank{i}", [P, T], F32)) for i in range(8)]

        raw_in = [sem(f"raw_in{i}") for i in range(4)]
        w_hi, w_lo = sem("w_hi"), sem("w_lo")
        pe_blk = sem("pe_blk")
        x_in, par_in, wf_in, c_in = (sem(n) for n in ("x_in", "par_in", "wf_in", "c_in"))
        modf_in = [sem(f"modf_in{i}") for i in range(4)]
        mod_in = [sem(f"mod_in{i}") for i in range(2)]
        mod_used = sem("mod_used")
        mod_set = sem("mod_set")
        consts = sem("consts")
        cact = sem("cact")
        dv = sem("dv")
        gp = sem("gp")
        ac = sem("ac")
        lb_mx, lb_ex = sem("lb_mx"), sem("lb_ex")
        x_sq, x_upd = sem("x_sq"), sem("x_upd")
        x_acc = sem("x_acc")
        n_sum, n_var, n_rst, n_dg, n_bc = (sem(n) for n in ("n_sum", "n_var", "n_rst", "n_dg", "n_bc"))
        h_t, h_hi, h_lo = (sem(n) for n in ("h_t", "h_hi", "h_lo"))
        ev_q, ev_f, ev_v, ev_g = (sem(n) for n in ("ev_q", "ev_f", "ev_v", "ev_g"))
        kf = sem("kf")
        lvl, sel, qup, kup, kread = (sem(n) for n in ("lvl", "sel", "qup", "kup", "kread"))
        off, o_pe, o_ev = (sem(n) for n in ("off", "o_pe", "o_ev"))
        g_sum, g_var, g_rst, g_dg, g_bc = (sem(n) for n in ("g_sum", "g_var", "g_rst", "g_dg", "g_bc"))
        hgo = sem("hgo")
        y_t, y_hi, y_lo = (sem(n) for n in ("y_t", "y_hi", "y_lo"))
        ff_r, ff_sq, ff_hi, ff_lo = (sem(n) for n in ("ff_r", "ff_sq", "ff_hi", "ff_lo"))
        f_w, f_wl, f_pe, f_ln, f_out, f_dram = (
            sem(n) for n in ("f_w", "f_wl", "f_pe", "f_ln", "f_out", "f_dram"))
        f_bc = [sem(f"f_bc{i}") for i in range(2)]
        fx_q, fx_v, fx_g = (sem(n) for n in ("fx_q", "fx_v", "fx_g"))
        fss = sem("fss")
        f_var, f_rst, f_nrm, f_tr, f_te = (sem(n) for n in ("f_var", "f_rst", "f_nrm", "f_tr", "f_te"))
        s_pe, s_ns, s_p, s_tr, s_pt, s_pv, s_rd, s_o = (
            sem(n) for n in ("s_pe", "s_ns", "s_p", "s_tr", "s_pt", "s_pv", "s_rd", "s_o"))
        ot_tr = sem("ot_tr")
        fy_t, fy_hi, fy_lo = (sem(n) for n in ("fy_t", "fy_hi", "fy_lo"))
        out_t_ready, out_done = sem("out_t_ready"), sem("out_done")

        NORM_SQ = [1, 2, 4, 5, 7]
        UPD = [0, KT, 3 * KT, 4 * KT]
        DG = [sqb, acc]
        UNITS = FH * TT
        full = [[i] for i in range(10)] + [[10, 11], [12, 13], [14, 15]]
        HALVES = [full] * (GROUPS - 1) + [[[0], [1], [2], [3]] + [[]] * 9]
        ENDS = [[[i // 2 for i in slot if i % 2] for slot in step] for step in HALVES]
        FHALVES = [[[u] for u in range(UNITS)]] * (GROUPS - 1) + [[[0], [1], [2], [3]] + [[]] * (UNITS - 4)]
        FENDS = [[[i // 2 for i in slot if i % 2] for slot in step] for step in FHALVES]
        TURN_Q = 12
        V, S, G, PE = nc.vector, nc.scalar, nc.gpsimd, nc.tensor

        def tile(t, i):
            return t[:, bass.ds(i, 1), :].rearrange("p o n -> p (o n)")

        def col(t, i):
            return t[:, bass.ds(i, 1)]

        def cols(t, i):
            return t[:, P * i:P * (i + 1)]

        def bank_of(s, u, what):
            return what + (4 if s == GROUPS - 1 and u % 2 and what < 2 else 0)

        block = keep.enter_context(nc.Block())

        @block.sync
        def _(sp):
            sp.dma_start(par[:, :], params).then_inc(par_in, 16)
            sp.dma_start(cb[:, :], c_row.partition_broadcast(P)).then_inc(c_in, 16)
            sp.dma_start(x[:, :, :], x_t).then_inc(x_in, 16)
            for i in range(4):
                sp.dma_start(modf[:, 4 * i:4 * i + 4, :],
                             mod_rows[4 * i:4 * i + 4].rearrange("m p k -> p m k")).then_inc(modf_in[i], 16)
            def weight(quad, j):
                sp.dma_start(raw[:, j, :], stream[bass.ds(quad * 4 + j, 1)].rearrange("b p n -> (b p) n")
                             ).then_inc(raw_in[j], 16)

            def modulation(m, s):
                sp.wait_ge(mod_used, m - 1)
                sp.dma_start(mring[:, s, :], mod_rows[bass.ds(m + 16, 1)].rearrange("b p n -> (b p) n")
                             ).then_inc(mod_in[s], 16)

            for j in range(4):
                weight(0, j)
            for j in range(4):
                sp.wait_ge(w_lo, j + 1)
                weight(1, j)
                if j < 2:
                    sp.dma_start(mring[:, j, :], mod_rows[16 + j]).then_inc(mod_in[j], 16)
                else:
                    modulation(j, j % 2)

            def both(first, end, ahead):
                with sp.Fori(first, end) as q:
                    for j in range(4):
                        sp.wait_ge(w_lo, (q - 1) * 4 + j + 1)
                        weight(q, j)
                        modulation((q - ahead) * 4 + j, j % 2)

            def alone(first, end):
                with sp.Fori(first, end) as q:
                    for j in range(4):
                        sp.wait_ge(w_lo, (q - 1) * 4 + j + 1)
                        weight(q, j)

            both(2, 9, 1)
            alone(9, 11)
            both(11, 23, 3)
            alone(23, 24)
            sp.dma_start(wf[:, :], w_forget).then_inc(wf_in, 16)
            alone(24, QUADS)
            for k in range(KT):
                sp.wait_ge(out_t_ready, k + 1)
                sp.dma_start(out_t[:, k, :], x[:, k, :]).then_inc(out_done, 16)
            sp.wait_ge(out_done, 16 * KT)

        @block.scalar
        def _(act):
            def hi_ahead(quad, j):
                act.wait_ge(pe_blk, quad * 4 + j + 1)
                act.wait_ge(raw_in[j], quad * 16 + 32)
                S.activation(whi[:, j, :], raw[:, j, :], ACT.Copy).then_inc(w_hi, 1)

            def norm(n, h, shift, first=False):
                for k in range(KT):
                    act.wait_ge(h_t, n * KT + k + 1)
                    S.activation(h[0][:, k, :], scr[k % 2][:, :], ACT.Identity,
                                 bias=mod[:, shift + k:shift + k + 1]).then_inc(h_hi, 1)

            act.wait_ge(c_in, 16)
            S.activation(cb[:, :], cb[:, :], ACT.Silu).then_inc(cact, 1)
            act.wait_ge(lb_mx, 1)
            S.activation(lbc[:, 24:48], lbc[:, 0:24], ACT.Exp).then_inc(lb_ex, 1)
            act.wait_ge(consts, 1)
            act.wait_ge(x_in, 16)
            for k in range(KT):
                if k:
                    act.wait_ge(x_acc, k)
                S.activation(sqb[:, :], x[:, k, :], ACT.Square).then_inc(x_sq, 1)
            for j in range(4):
                act.wait_ge(raw_in[j], 16)
                S.activation(whi[:, j, :], raw[:, j, :], ACT.Copy).then_inc(w_hi, 1)
            norm(0, h0, SH1)

            def hg_dense(s, b):
                n = 6 + 8 * s + b
                g, j = s + 1, b % 2
                at = 2 * (g % 2) + j
                act.wait_ge(pe_blk, n + 1)
                if b < 2:
                    S.activation(hgate[:, j, :], ps[6 + j][:, :], ACT.Silu).then_inc(ev_g, 1)
                elif b < 4:
                    if g >= 2:
                        act.wait_ge(y_t, 2 * (g - 2) + 2)
                    S.activation(hq[:, at, :], ps[4 + j][:, :], ACT.Silu).then_inc(ev_q, 1)
                elif b < 6:
                    S.activation(hf[:, at, :], ps[6 + j][:, :], ACT.Sigmoid)
                    S.activation(hk[:, at, :], ps[6 + j][:, :], ACT.Sigmoid, scale=-1.0).then_inc(ev_f, 1)
                elif b == 7:
                    for i in range(2):
                        S.activation(hv[:, 2 * i:2 * i + 2, GW * (g % 2):GW * (g % 2) + GW],
                                     ps[4 + i][:, :].rearrange("p (t v) -> p t v", v=GW), ACT.Copy).then_inc(ev_v, 1)
                hi_ahead(n // 4, n % 4)

            def hg_core(s, slot):
                p0 = 2 * (s % 2)
                if slot == 9:
                    for j in range(GH):
                        act.wait_ge(lvl, 20 * s + 18 + 2)
                        S.activation(hf[:, p0 + j, :], ps[j][:, :], ACT.Copy)
                        S.activation(hk[:, p0 + j, 256:512], ps[2][:, 256 * j:256 * j + 256], ACT.Copy).then_inc(off, 1)
                elif slot == 10:
                    for j in range(GH):
                        act.wait_ge(o_pe, 2 * s + j + 1)
                        S.activation(hk[:, p0 + j, :], ps[3 - j][:, :], ACT.Square)
                        S.activation(hq[:, p0 + j, :], ps[3 - j][:, :], ACT.Copy).then_inc(o_ev, 1)
                elif slot == 12:
                    for j in range(GH):
                        act.wait_ge(y_t, 2 * s + j + 1)
                        S.activation(y0[0][:, 2 * s + j, :], scr[j][:, :], ACT.Copy).then_inc(y_hi, 1)

            for b in range(2, 8):
                hg_dense(-1, b)
            for s in range(GROUPS):
                for slot, ends in enumerate(ENDS[s]):
                    hg_core(s, slot)
                    for b in ends:
                        hg_dense(s, b)

            def residual(quads, q0, per, sq0, first):
                def body(q, last):
                    for j in range(4):
                        if not last:
                            hi_ahead(q0 + q, j)
                        if j % per == per - 1:
                            n = q * (4 // per) + j // per
                            act.wait_ge(x_upd, sq0 + n + 1)
                            act.wait_ge(x_acc, sq0 + n + KT)
                            S.activation(sqb[:, :], tile(x, n), ACT.Square).then_inc(x_sq, 1)
                n_loop = quads - (1 if first else 0)
                with act.Fori(0, n_loop) as q:
                    body(q, False)
                if first:
                    body(quads - 1, True)

            def mlp(layer, a, n_norm, h, sq0):
                base = layer * LAYER_QUADS + Q_MLP
                for half in range(2):
                    with act.Fori(0, 4) as q:
                        for j in range(4):
                            act.wait_ge(pe_blk, (q + base + 8 * half) * 4 + j + 1)
                            ff_n = (q + 4 * half) * 4 + j + 32 * layer
                            if layer or half or j >= 2:
                                act.wait_ge(ff_lo, ff_n - 1)
                            S.activation(scr[j % 2][:, :], ps[j][:, :], ACT.Relu).then_inc(ff_r, 1)
                            hi_ahead(q + base + 8 * half, j)
                            act.wait_ge(ff_sq, ff_n + 1)
                            S.activation(tile(a[0], q * 4 + j), scr[j % 2][:, :], ACT.Copy).then_inc(ff_hi, 1)
                    residual(4, base + 8 * half + 4, 2, sq0 + KT * half, layer == 1 and half == 1)

            residual(2, Q_OUT, 1, 0, False)
            norm(1, h1, SH2)
            mlp(0, a0, 1, h1, KT)
            act.wait_ge(wf_in, 16)
            S.activation(wfs[0][:, :], wf[:, :], ACT.Copy).then_inc(f_w, 1)
            norm(2, h2, 48 + SH1)
            act.wait_ge(f_pe, 1)
            S.activation(sqb[:, :], ps[0][:, :], ACT.Abs, bias=par[:, C_BF:C_BF + 1]).then_inc(ac, 1)
            act.wait_ge(ac, 1)
            S.activation(sqb[:, :], sqb[:, :], ACT.Exp, scale=-1.0).then_inc(ac, 1)
            act.wait_ge(ac, 2)
            S.activation(sqb[:, :], sqb[:, :], ACT.Ln, bias=1.0).then_inc(f_ln, 1)
            act.wait_ge(f_out, 1)
            act.dma_start(fscr, acc[0:HEADS, :]).then_inc(f_dram, 16)
            act.wait_ge(f_dram, 16)

            L = LAYER_QUADS

            def forget(g):
                act.dma_start(fb[:, FH * (g % 2):FH * (g % 2) + FH, :],
                              fscr[FH * g:FH * g + FH, :].partition_broadcast(P)).then_inc(f_bc[g % 2], 16)

            def fox_dense(s, b):
                n = 4 * L + 6 + 8 * s + b
                g = s + 1
                act.wait_ge(pe_blk, n + 1)
                if b < 2:
                    S.activation(gs[:, b, :], ps[6 + b][:, :], ACT.Sigmoid).then_inc(fx_g, 1)
                elif b in (3, 5):
                    w = (b - 3) // 2
                    for i in range(2):
                        c = 4 * g + 2 * w + i
                        act.wait_ge(fss, c)
                        if g:
                            act.wait_ge(f_tr, 4 * (g - 1) + 2 * w + 2)
                        S.activation(sqb[:, :], ps[4 + 2 * w + i][:, :], ACT.Square)
                        S.activation(qkt[w][:, 2 * i:2 * i + 2, :],
                                     ps[4 + 2 * w + i][:, :].rearrange("p (t v) -> p t v", v=GW),
                                     ACT.Copy).then_inc(fx_q, 1)
                elif b == 7:
                    for i in range(2):
                        S.activation(vt[:, 2 * i:2 * i + 2, GW * (g % 2):GW * (g % 2) + GW],
                                     ps[4 + i][:, :].rearrange("p (t v) -> p t v", v=GW), ACT.Copy).then_inc(fx_v, 1)
                hi_ahead(n // 4, n % 4)

            def turned_out(g, w):
                scale = (qkw[:, 0:1], par[:, C_KN:C_KN + 1])[w]
                for f in range(2):
                    act.wait_ge(f_tr, 4 * g + 2 * w + f + 1)
                    S.activation(qkT[w][:, 2 * (g % 2) + f, :], ps[3][:, :], ACT.Copy, scale=scale).then_inc(f_te, 1)

            def y_upper(s):
                for f in range(2):
                    act.wait_ge(fy_t, 2 * s + f + 1)
                    S.activation(y1[0][:, 2 * s + f, :], (acc, sqb)[f][:, :], ACT.Copy).then_inc(fy_hi, 1)

            forget(0)
            for b in range(2, 8):
                fox_dense(-1, b)
            turned_out(0, 0)
            turned_out(0, 1)
            for s in range(GROUPS):
                if s + 1 < GROUPS:
                    if s >= 1:
                        act.wait_ge(s_ns, UNITS * s)
                    forget(s + 1)
                for u in range(UNITS):
                    n, c = P * (u % TT + 1), UNITS * s + u
                    act.wait_ge(s_ns, c + 1)
                    if c >= 2:
                        act.wait_ge(s_tr, c - 1)
                    S.activation(prob[:, u % 2, 0:n], scr[u % 2][:, 0:n], ACT.Exp, scale=-1.0,
                                 bias=small[:, c:c + 1], accum_out=den[:, c:c + 1]).then_inc(s_p, 1)
                    if s and u == 1:
                        y_upper(s - 1)
                    if s + 1 < GROUPS and u == TURN_Q + 1:
                        turned_out(s + 1, 0)
                    for b in FENDS[s][u]:
                        fox_dense(s, b)
                if s + 1 < GROUPS:
                    turned_out(s + 1, 1)
            y_upper(GROUPS - 1)
            residual(2, L + Q_OUT, 1, 3 * KT, False)
            norm(3, h3, 48 + SH2)
            mlp(1, a1, 3, h3, 4 * KT)

        @block.gpsimd
        def _(pool):
            G.memset(ident[:, :], 0.0).then_inc(gp, 1)
            G.memset(mhalf[:, :], -0.5).then_inc(gp, 1)
            G.memset(ones[:, :], 1.0)
            G.memset(meand[:, 0:1], 1.0 / D)
            G.memset(meand[:, 1:2], 1.0 / P)
            pool.wait_ge(gp, 1)
            G.affine_select(out=ident[:, :], in_=ident[:, :], compare_op=ALU.not_equal, fill=1.0,
                            base=0, pattern=[[-1, P]], channel_multiplier=1).then_inc(gp, 1)
            pool.wait_ge(gp, 3)
            G.tensor_copy(identb[:, :], ident[:, :]).then_inc(gp, 1)
            G.memset(causal[:, :], 0.0).then_inc(gp, 1)
            pool.wait_ge(gp, 5)
            G.affine_select(out=causal[:, :], in_=causal[:, :], compare_op=ALU.is_ge, fill=-3e38,
                            base=0, pattern=[[-1, P]], channel_multiplier=1).then_inc(gp, 1)
            n = 6
            for lv in range(MASKED):
                pool.wait_ge(gp, n)
                if lv:
                    m = 1 << (lv - 1)
                    nb = P // (2 * m)
                    v = sqb[:, 0:P].rearrange("p (b h m) -> p b h m", h=2, m=m)
                    G.memset(v[:, :, 0, :], 0.0)
                    G.memset(v[:, :, 1, :], 1.0).then_inc(gp, 1)
                    pool.wait_ge(gp, n + 1)
                    G.affine_select(out=v[:, :, 1, :], in_=v[:, :, 1, :], compare_op=ALU.is_ge, fill=0.0,
                                    base=0, pattern=[[-2 * m, nb], [0, m]], channel_multiplier=1).then_inc(gp, 1)
                    pool.wait_ge(gp, n + 2)
                    G.affine_select(out=v[:, :, 1, :], in_=v[:, :, 1, :], compare_op=ALU.is_gt, fill=0.0,
                                    base=m, pattern=[[2 * m, nb], [0, m]], channel_multiplier=-1).then_inc(gp, 1)
                    pool.wait_ge(gp, n + 3)
                    G.tensor_copy(masks[:, lv, :], sqb[:, 0:P]).then_inc(gp, 1)
                    n += 4
            pool.wait_ge(gp, n)
            G.memset(sqb[:, 0:1], 0.0).then_inc(consts, 1)

            def lo(quad_plus, j):
                pool.wait_ge(w_hi, quad_plus * 4 + j + 1)
                G.tensor_tensor(wlo[:, j, :], raw[:, j, :], whi[:, j, :].bitcast(F32), ALU.subtract).then_inc(w_lo, 1)

            def root(ready, ready_at, n, done, at=0):
                pool.wait_ge(ready, ready_at)
                G.tensor_tensor(rst[:, at:at + n], ssq[:, at:at + n], mhalf[:, 0:n], ALU.pow).then_inc(done, 1)

            root(n_var, 1, TT, n_rst)
            for j in range(4):
                lo(0, j)

            def lo_ahead(n):
                lo(n // 4 + 1, n % 4)

            for b in range(6):
                lo_ahead(b)
            for s in range(GROUPS):
                p0 = 2 * (s % 2)
                for slot, ends in enumerate(ENDS[s]):
                    if 1 <= slot < SPLITS - 1:
                        m = 1 << (slot - 1)
                        shape = [P, T // (2 * m), m]
                        for j in range(GH):
                            kv = hk[:, p0 + j, :].rearrange("p (b h m) -> p b h m", h=2, m=m)
                            tv = hf[:, p0 + j, :].rearrange("p (b h m) -> p b h m", h=2, m=m)
                            pool.wait_ge(lvl, 20 * s + 2 * slot + j + 1)
                            last = slot == SPLITS - 2
                            G.tensor_tensor(kv[:, :, 0, :], kv[:, :, 0, :], tv[:, :, 1, 0:1].broadcast_to(shape),
                                            ALU.mult).then_inc(kup if last else kread, 1)
                            if not last:
                                pool.wait_ge(kread, 14 * s + 2 * (slot - 1) + j + 1)
                                pool.wait_ge(qup, 18 * s + 2 * slot + j + 1)
                                G.tensor_tensor(tv[:, :, 0, 0], tv[:, :, 0, 0], tv[:, :, 1, 0],
                                                ALU.mult).then_inc(kup, 1)
                    if slot == 11:
                        root(g_var, s + 1, 4 * GH, g_rst)
                    for b in ends:
                        lo_ahead(6 + 8 * s + b)
            with pool.Fori(Q_OUT + 1, Q_OUT + 3) as q:
                for j in range(4):
                    lo(q, j)
            root(n_var, 2, TT, n_rst)
            with pool.Fori(Q_MLP + 1, LAYER_QUADS + 1) as q:
                for j in range(4):
                    lo(q, j)
            root(n_var, 3, TT, n_rst)
            L = LAYER_QUADS
            for s in range(-1, GROUPS):
                for b in range(2 if s < 0 else 0, 2 if s == GROUPS - 1 else 8):
                    lo_ahead(4 * L + 6 + 8 * s + b)
                    if b in (3, 5):
                        w = (b - 3) // 2
                        root(f_var, 2 * (s + 1) + w + 1, 16, f_rst, 16 * w)
            with pool.Fori(L + Q_OUT + 1, L + Q_OUT + 3) as q:
                for j in range(4):
                    lo(q, j)
            root(n_var, 4, TT, n_rst)
            with pool.Fori(L + Q_MLP + 1, QUADS) as q:
                for j in range(4):
                    lo(q, j)
            root(n_var, 5, TT, n_rst)

        @block.tensor
        def _(pe):
            def split(quad, j):
                pe.wait_ge(w_hi, quad * 4 + j + 1)
                pe.wait_ge(w_lo, quad * 4 + j + 1)

            def product(out, w, k, hh, first, last):
                wh, wl = whi[:, w, P * k:P * k + P], wlo[:, w, P * k:P * k + P]
                PE.matmul(out, wh, hh[0], start=first, stop=False)
                PE.matmul(out, wh, hh[1], start=False, stop=False)
                return PE.matmul(out, wl, hh[0], start=False, stop=last)

            def feature_block(quad, j, bank, h, k0=0, first=True, last=True, ready=None):
                split(quad, j)
                for k in range(KT):
                    if ready is not None:
                        pe.wait_ge(h_lo, ready + k + 1)
                    mm = product(ps[bank][:, :], j, k, [h[0][:, k0 + k, :], h[1][:, k0 + k, :]],
                                 first and k == 0, last and k == KT - 1)
                mm.then_inc(pe_blk, 1)

            def norm(n):
                pe.wait_ge(x_acc, KT * NORM_SQ[n])
                for t in range(TT):
                    mm = PE.matmul(ps[6][:, t:t + 1], cols(acc, t), meand[:, 0:1], start=True, stop=True)
                mm.then_inc(n_sum, 1)
                pe.wait_ge(n_dg, n + 1)
                for t in range(TT):
                    mm = PE.matmul(cols(ps[7], t), ones[:, :], cols(sqb, t), start=True, stop=True)
                mm.then_inc(n_bc, 1)

            pe.wait_ge(consts, 1)
            norm(0)

            def half_feature(n, half, bank, h, ready=None):
                if half == 0:
                    split(n // 4, n % 4)
                for k in range(4 * half, 4 * half + 4):
                    if ready is not None:
                        pe.wait_ge(h_lo, ready + k + 1)
                    mm = product(ps[bank][:, :], n % 4, k, [h[0][:, k, :], h[1][:, k, :]], k == 0, k == KT - 1)
                if half:
                    mm.then_inc(pe_blk, 1)

            def quarter_token(n, quarter, bank, h):
                j = n % 4
                if quarter % 2 == 0:
                    split(n // 4, j)
                for k in (2 * quarter, 2 * quarter + 1):
                    w0 = slice(GW * (k % 4), GW * (k % 4) + GW)
                    for t in range(TT):
                        o = ps[bank + t // 2][:, GW * (t % 2):GW * (t % 2) + GW]
                        hh, hl = cols(h[0][:, k, :], t), cols(h[1][:, k, :], t)
                        PE.matmul(o, hh, whi[:, j, w0], start=k == 0 and t % 2 == 0, stop=False, skip_group_check=True)
                        PE.matmul(o, hl, whi[:, j, w0], start=False, stop=False, skip_group_check=True)
                        mm = PE.matmul(o, hh, wlo[:, j, w0], start=False, stop=k == KT - 1, skip_group_check=True)
                if quarter % 2:
                    mm.then_inc(pe_blk, 1)

            def hg_half(s, i, ready=None):
                b, half = i // 2, i % 2
                n, g, j = 6 + 8 * s + b, s + 1, b % 2
                if half == 0:
                    if b < 2:
                        pe.wait_ge(ev_f, 2 * s + j + 1)
                    elif b < 4 and g:
                        pe.wait_ge(ev_v, 2 * (g - 1) + 2)
                    elif b in (4, 5) and g:
                        pe.wait_ge(ev_g, 2 * s + j + 1)
                    elif b == 6:
                        pe.wait_ge(ev_q, 2 * g + 2)
                if b < 6:
                    half_feature(n, half, (6, 4, 6)[b // 2] + j, h0, ready)
                else:
                    quarter_token(n, i - 12, 4, h0)

            for i in range(4, 16):
                hg_half(-1, i, 0 if i < 6 else None)

            def hg_core(s, slot):
                p0 = 2 * (s % 2)
                for j in range(GH):
                    kk, qq = hk[:, p0 + j, :], hq[:, p0 + j, :]
                    if slot < SPLITS:
                        lv = slot
                        if lv == 0:
                            pe.wait_ge(kf, 2 * s + j + 1)
                            pe.wait_ge(ev_q, 2 * s + j + 1)
                            pe.wait_ge(y_t, 2 * s)
                        else:
                            pe.wait_ge(qup, 18 * s + 2 * (lv - 1) + j + 1)
                            if lv >= 2:
                                pe.wait_ge(kup, 16 * s + 2 * (lv - 2) + j + 1)
                            if lv <= MASKED:
                                pe.wait_ge(sel, 16 * s + 2 * (lv - 1) + j + 1)
                        if lv < MASKED:
                            for t in range(TT):
                                mm = PE.matmul(cols(ps[j], t), cols(kk, t), cols(qq, t), start=True, stop=True)
                        elif lv == 8:
                            PE.matmul(cols(ps[j], 0), cols(kk, 0), cols(qq, 1), start=True, stop=True)
                            mm = PE.matmul(cols(ps[j], 3), cols(kk, 2), cols(qq, 3), start=True, stop=True)
                        else:
                            PE.matmul(ps[j][:, 128:384], cols(kk, 0), qq[:, 256:512], start=True, stop=True)
                            mm = PE.matmul(ps[2][:, 256 * j:256 * j + 256], cols(kk, 1), qq[:, 256:512],
                                           start=True, stop=True)
                        mm.then_inc(lvl, 1)
                    elif slot == 10:
                        pe.wait_ge(off, 2 * s + GH)
                        if j == 0:
                            pe.wait_ge(ev_v, 2 * s + 2)
                        o, at = ps[3 - j], p0 + j
                        v = [hv[:, t, P * at:P * at + P] for t in range(TT)]
                        f_, k_ = hf[:, at, :], hk[:, at, :]
                        parts = [(0, P, v[0], cols(adiag[:, j, :], 0)), (P, T, v[0], f_[:, 0:384]),
                                 (256, T, v[1], k_[:, 256:512]), (384, T, v[2], f_[:, 384:512])]
                        parts += [(P * t, P * t + P, v[t], cols(adiag[:, j, :], t)) for t in range(1, TT)]
                        for i, (a, b, lhs, rhs) in enumerate(parts):
                            mm = PE.matmul(o[:, a:b], lhs, rhs, start=i == 0, stop=i == len(parts) - 1,
                                           skip_group_check=True)
                        mm.then_inc(o_pe, 1)
                    elif slot == 11:
                        pe.wait_ge(o_ev, 2 * s + j + 1)
                        for t in range(TT):
                            mm = PE.matmul(ps[0][:, 4 * j + t:4 * j + t + 1], cols(kk, t), meand[:, 1:2],
                                           start=True, stop=True)
                        if j == GH - 1:
                            mm.then_inc(g_sum, 1)
                    else:
                        pe.wait_ge(g_dg, 2 * s + j + 1)
                        for t in range(TT):
                            mm = PE.matmul(cols(ps[1 + 2 * j], t), ones[:, :], cols(DG[j], t), start=True, stop=True)
                        mm.then_inc(g_bc, 1)

            for s in range(GROUPS):
                for slot, halves in enumerate(HALVES[s]):
                    hg_core(s, slot)
                    for i in halves:
                        hg_half(s, i)

            def w_out(quad, y, y_done, upd0):
                pe.wait_ge(*y_done)
                with pe.Fori(0, 2) as q:
                    for j in range(4):
                        pe.wait_ge(x_upd, q * 4 + (upd0 + j - 3)) if upd0 + j - 3 > 0 else (
                            pe.wait_ge(x_upd, q * 4))
                        feature_block(q + quad, j, j, y)

            def mlp(layer, h, a, n):
                base = layer * LAYER_QUADS + Q_MLP
                for half in range(2):
                    with pe.Fori(0, 4) as q:
                        for j in range(4):
                            pe.wait_ge(ff_r, q * 4 + (32 * layer + 16 * half + j - 3 if layer or half or j == 3 else 0))
                            feature_block(q + base + 8 * half, j, j, h, ready=KT * n if j == 0 else None)
                    with pe.Fori(0, 4) as q:
                        for j in range(4):
                            if j % 2 == 0:
                                pe.wait_ge(x_upd, q * 2 + (UPD[2 * layer + 1] + KT * half + j // 2 - 1))
                            if j == 0:
                                pe.wait_ge(ff_lo, 32 * layer + 16 * (half + 1))
                            feature_block(q + base + 8 * half + 4, j, 4 + j // 2, a, k0=KT * (j % 2),
                                          first=j % 2 == 0, last=j % 2 == 1)

            w_out(Q_OUT, y0, (y_lo, 8), 0)
            norm(1)
            mlp(0, h1, a0, 1)
            norm(2)
            pe.wait_ge(f_wl, 1)
            for k in range(KT):
                pe.wait_ge(h_lo, 2 * KT + k + 1)
                wh, wl = cols(wfs[0], k), cols(wfs[1], k)
                PE.matmul(ps[0][:, :], wh, h2[0][:, k, :], start=k == 0, stop=False)
                PE.matmul(ps[0][:, :], wh, h2[1][:, k, :], start=False, stop=False)
                mm = PE.matmul(ps[0][:, :], wl, h2[0][:, k, :], start=False, stop=k == KT - 1)
            mm.then_inc(f_pe, 1)
            L = LAYER_QUADS
            pe.wait_ge(f_out, 1)

            def fox_half(s, i):
                b, half = i // 2, i % 2
                n, g = 4 * L + 6 + 8 * s + b, s + 1
                if half == 0:
                    if b < 2:
                        pe.wait_ge(fx_q, 4 * s + 4)
                    elif b == 2 and g:
                        pe.wait_ge(fx_v, 2 * g)
                    elif b == 4 and g:
                        pe.wait_ge(fx_g, 2 * g)
                    elif b == 6:
                        pe.wait_ge(fx_q, 4 * g + 2)
                if b < 2:
                    half_feature(n, half, 6 + b, h2)
                else:
                    quarter_token(n, (i - 4) % 4, (4, 6, 4)[(b - 2) // 2], h2)

            def turn(g, w):
                pe.wait_ge(f_nrm, 4 * g + 2 * w + 2)
                for f in range(2):
                    if g or w or f:
                        pe.wait_ge(f_te, 4 * g + 2 * w + f)
                    for t in range(TT):
                        mm = PE.transpose(cols(ps[3], t), cols(qkt[w][:, t, :], f), ident[:, :])
                    mm.then_inc(f_tr, 1)

            def scores(s, u):
                a, i = divmod(u, TT)
                r, f = DH * (a % 2), 2 * (s % 2) + a // 2
                c = UNITS * s + u
                if c >= 1:
                    pe.wait_ge(s_ns, c if s < GROUPS - 1 or u < 2 else c - 1)
                n = P * (i + 1)
                o = ps[bank_of(s, u, 0)]
                PE.matmul(o[:, 0:n], qkT[0][r:r + DH, f, P * i:P * i + P], qkT[1][r:r + DH, f, 0:n],
                          start=True, stop=False, skip_group_check=True)
                PE.matmul(o[:, n - P:n], identb[:, :], causal[:, :],
                          start=False, stop=True, skip_group_check=True).then_inc(s_pe, 1)

            def transposes(s, u):
                c = UNITS * s + u
                pe.wait_ge(s_p, c + 1)
                if c >= 1:
                    pe.wait_ge(s_pt, c if s < GROUPS - 1 or u < 2 else c - 1)
                for t in range(u % TT + 1):
                    mm = PE.transpose(cols(ps[bank_of(s, u, 1)], t), cols(prob[:, u % 2, :], t), ident[:, :])
                mm.then_inc(s_tr, 1)

            def values(s, u):
                a, i = divmod(u, TT)
                pe.wait_ge(s_pt, UNITS * s + u + 1)
                if i == 0:
                    pe.wait_ge(s_o, FH * s + a)
                    pe.wait_ge(fy_t, 2 * s)
                v0 = GW * (s % 2) + DH * a
                for t in range(i + 1):
                    mm = PE.matmul(ps[2][:, DH * i:DH * i + DH], cols(pT[:, u % 2, :], t),
                                   vt[:, t, v0:v0 + DH], start=t == 0, stop=t == i)
                mm.then_inc(s_pv, 1)

            def turn_o(s):
                pe.wait_ge(s_o, FH * s + FH)
                for f in range(2):
                    for t in range(TT):
                        mm = PE.transpose(cols(ps[2 + f], t), cols(ot[:, t, :], f), ident[:, :])
                    mm.then_inc(ot_tr, 1)

            for i in range(4, 16):
                fox_half(-1, i)
            turn(0, 0)
            turn(0, 1)
            for s in range(GROUPS):
                pe.wait_ge(f_te, 4 * s + 4)
                pe.wait_ge(fx_v, 2 * s + 2)
                scores(s, 0)
                for u in range(UNITS):
                    if u + 1 < UNITS:
                        scores(s, u + 1)
                    transposes(s, u)
                    for i in FHALVES[s][u]:
                        fox_half(s, i)
                    if s and u == 0:
                        turn_o(s - 1)
                    if u >= 1:
                        values(s, u - 1)
                    if s + 1 < GROUPS and u == TURN_Q:
                        turn(s + 1, 0)
                values(s, UNITS - 1)
                if s + 1 < GROUPS:
                    turn(s + 1, 1)
                else:
                    turn_o(s)
            w_out(L + Q_OUT, y1, (fy_lo, 8), UPD[2])
            norm(3)
            mlp(1, h3, a1, 3)
            norm(4)

        @block.vector
        def _(dve):
            chain = [0]

            def link(ins):
                chain[0] += 1
                ins.then_inc(dv, 1)
                dve.wait_ge(dv, chain[0])

            def eps_var(bank_cols, n, at=0):
                return V.tensor_scalar(ssq[:, at:at + n], bank_cols, EPS, None, ALU.add)

            def diagonals(dst, roots):
                return V.tensor_tensor(dst.rearrange("p (t q) -> p t q", q=P),
                                       ident[:, :].unsqueeze(1).broadcast_to([P, TT, P]),
                                       roots.unsqueeze(2).broadcast_to([P, TT, P]), ALU.mult)

            def root_of_x(n):
                dve.wait_ge(n_sum, n + 1)
                eps_var(ps[6][:, 0:TT], TT).then_inc(n_var, 1)
                dve.wait_ge(n_rst, n + 1)
                diagonals(sqb[:, :], rst[:, 0:TT]).then_inc(n_dg, 1)
                dve.wait_ge(n_bc, n + 1)

            def norm(n, h, gain0, shift, rooted=False):
                if not rooted:
                    root_of_x(n)

                def t_of(k):
                    if k >= 2:
                        dve.wait_ge(h_lo, n * KT + k - 1)
                    V.scalar_tensor_tensor(out=scr[k % 2][:, :], in0=x[:, k, :], scalar=gain[:, gain0 + k:gain0 + k + 1],
                                           in1=ps[7][:, :], op0=ALU.mult, op1=ALU.mult).then_inc(h_t, 1)

                t_of(0)
                for k in range(KT):
                    if k + 1 < KT:
                        t_of(k + 1)
                    dve.wait_ge(h_hi, n * KT + k + 1)
                    V.scalar_tensor_tensor(out=h[1][:, k, :], in0=scr[k % 2][:, :],
                                           scalar=mod[:, shift + k:shift + k + 1],
                                           in1=h[0][:, k, :].bitcast(F32), op0=ALU.add,
                                           op1=ALU.subtract).then_inc(h_lo, 1)

            def modulation(mq, j):
                s = j % 2
                dve.wait_ge(mod_in[s], mq * 32 + 16 * (j // 2 + 1))
                if j == 0:
                    dve.wait_ge(mod_set, mq)
                V.tensor_tensor_reduce(out=mring[:, s, :], in0=mring[:, s, :], in1=cb[:, :], scale=1.0, scalar=0.0,
                                       op0=ALU.mult, op1=ALU.add, accum_out=dots[:, j:j + 1]).then_inc(mod_used, 1)
                if j == 3:
                    dve.wait_ge(mod_used, mq * 4 + 4)
                    V.tensor_copy(mod[:, bass.ds(mq * 4 + 16, 4)], dots[:, :]).then_inc(mod_set, 1)

            def add_bias(lo_, hi_):
                link(V.tensor_tensor(mod[:, lo_:hi_], mod[:, lo_:hi_], par[:, C_BMOD + lo_:C_BMOD + hi_], ALU.add))

            def gains(i, norm_col, scale_col):
                link(V.scalar_tensor_tensor(out=gain[:, KT * i:KT * i + KT], in0=mod[:, scale_col:scale_col + KT],
                                            scalar=1.0, in1=par[:, norm_col:norm_col + KT],
                                            op0=ALU.add, op1=ALU.mult))

            def half_y(n, t, hi_sem, lo_sem, y):
                dve.wait_ge(hi_sem, n + 1)
                V.tensor_tensor(y[1][:, n, :], t[:, :], y[0][:, n, :].bitcast(F32), ALU.subtract).then_inc(lo_sem, 1)

            dve.wait_ge(par_in, 16)
            lb = [par[:, C_LB + KT * i:C_LB + KT * i + KT] for i in range(3)]
            link(V.tensor_tensor(small[:, 0:8], lb[0], lb[1], ALU.max))
            link(V.tensor_tensor(small[:, 8:16], small[:, 0:8], lb[2], ALU.max))
            for i in range(3):
                ins = V.tensor_tensor(lbc[:, KT * i:KT * i + KT], lb[i], small[:, 8:16], ALU.subtract)
            ins.then_inc(lb_mx, 1)
            V.tensor_scalar(qkw[:, :], par[:, C_QN:C_QN + 1], DH ** -0.5, None, ALU.mult)
            dve.wait_ge(lb_ex, 1)
            link(V.tensor_tensor(small[:, 0:8], lbc[:, 32:40], lbc[:, 40:48], ALU.add))
            link(V.tensor_tensor(small[:, 8:16], small[:, 0:8], lbc[:, 24:32], ALU.add))
            link(V.reciprocal(small[:, 16:24], small[:, 8:16]))
            V.tensor_tensor(lbc[:, 0:8], lbc[:, 24:32], small[:, 16:24], ALU.mult)
            link(V.tensor_tensor(lbc[:, 8:16], small[:, 0:8], small[:, 16:24], ALU.mult))

            dve.wait_ge(consts, 1)
            link(V.memset(acc[:, :], 0.0))
            for k in range(KT):
                dve.wait_ge(x_sq, k + 1)
                if k:
                    dve.wait_ge(x_acc, k)
                V.tensor_tensor(acc[:, :], acc[:, :], sqb[:, :], ALU.add).then_inc(x_acc, 1)
            root_of_x(0)
            dve.wait_ge(cact, 1)
            for m in range(16):
                if m % 4 == 0:
                    dve.wait_ge(modf_in[m // 4], 16)
                ins = V.tensor_tensor_reduce(out=modf[:, m, :], in0=modf[:, m, :], in1=cb[:, :], scale=1.0, scalar=0.0,
                                             op0=ALU.mult, op1=ALU.add, accum_out=mod[:, m:m + 1])
            link(ins)
            add_bias(0, 16)
            gains(0, C_N1, SC1)
            norm(0, h0, 0, SH1, rooted=True)

            def hg_dense(s, b):
                n, g, j = 6 + 8 * s + b, s + 1, b % 2
                if b in (4, 5):
                    at = 2 * (g % 2) + j
                    dve.wait_ge(ev_f, 2 * g + j + 1)
                    c = 2 * g + j
                    V.tensor_scalar(hf[:, at, :], hf[:, at, :], lbc[:, 8 + c:9 + c], lbc[:, c:c + 1],
                                    ALU.mult, ALU.add)
                    V.tensor_scalar(hk[:, at, :], hk[:, at, :], lbc[:, 8 + c:9 + c], None, ALU.mult).then_inc(kf, 1)
                modulation(n // 4, n % 4)

            def hg_core(s, slot):
                p0 = 2 * (s % 2)
                lv, m = slot, 1 << max(slot - 1, 0)
                for j in range(GH):
                    q, f = hq[:, p0 + j, :], hf[:, p0 + j, :]
                    if slot < SPLITS - 1:
                        dve.wait_ge(lvl, 20 * s + 2 * lv + j + 1)
                        bank = ps[j][:, :].rearrange("p (t q) -> p t q", q=P)
                        ad = adiag[:, j, :].rearrange("p (t q) -> p t q", q=P)
                        if lv == 0:
                            V.tensor_tensor(q, q, f, ALU.mult).then_inc(qup, 1)
                            V.tensor_tensor(ad, bank, ident[:, :].unsqueeze(1).broadcast_to([P, TT, P]),
                                            ALU.mult).then_inc(sel, 1)
                            continue
                        qv = q.rearrange("p (b h m) -> p b h m", h=2, m=m)
                        tv = f.rearrange("p (b h m) -> p b h m", h=2, m=m)
                        V.tensor_tensor(qv[:, :, 1, :], qv[:, :, 1, :],
                                        tv[:, :, 0, 0:1].broadcast_to([P, T // (2 * m), m]), ALU.mult).then_inc(qup, 1)
                        if lv < MASKED:
                            V.copy_predicated(ad, masks[:, lv, :].unsqueeze(1).broadcast_to([P, TT, P]),
                                              bank).then_inc(sel, 1)
                    elif slot == 10:
                        dve.wait_ge(o_ev, 2 * s + j + 1)
                        dve.wait_ge(ev_g, 2 * s + j + 1)
                        V.tensor_tensor(hgate[:, j, :], hgate[:, j, :], q, ALU.mult).then_inc(hgo, 1)
                if slot == 11:
                    dve.wait_ge(g_sum, s + 1)
                    eps_var(ps[0][:, 0:4 * GH], 4 * GH).then_inc(g_var, 1)
                    dve.wait_ge(g_rst, s + 1)
                    for j in range(GH):
                        diagonals(DG[j][:, :], rst[:, 4 * j:4 * j + 4]).then_inc(g_dg, 1)
                elif slot == 12:
                    for j in range(GH):
                        dve.wait_ge(g_bc, 2 * s + j + 1)
                        dve.wait_ge(hgo, 2 * s + j + 1)
                        if s:
                            dve.wait_ge(y_lo, 2 * s + j - 1)
                        V.scalar_tensor_tensor(out=scr[j][:, :], in0=hgate[:, j, :], scalar=par[:, C_GN:C_GN + 1],
                                               in1=ps[1 + 2 * j][:, :], op0=ALU.mult, op1=ALU.mult).then_inc(y_t, 1)
                    for j in range(GH):
                        half_y(2 * s + j, scr[j], y_hi, y_lo, y0)

            for b in range(2, 8):
                hg_dense(-1, b)
            for s in range(GROUPS):
                for slot, ends in enumerate(ENDS[s]):
                    hg_core(s, slot)
                    for b in ends:
                        hg_dense(s, b)

            def residual(quads, q0, per, gate, upd0, start_at):
                link(V.memset(acc[:, :], 0.0))
                def add(n, base):
                    dve.wait_ge(x_sq, n + (base + 1))
                    dve.wait_ge(x_acc, n + base)
                    V.tensor_tensor(acc[:, :], acc[:, :], sqb[:, :], ALU.add).then_inc(x_acc, 1)
                with dve.Fori(0, quads) as q:
                    for j in range(0, 4, per):
                        n = q * (4 // per) + j // per
                        bank = j if per == 1 else 4 + j // 2
                        dve.wait_ge(pe_blk, (q + q0) * 4 + j + per)
                        V.scalar_tensor_tensor(out=tile(x, n), in0=ps[bank][:, :], scalar=col(mod, n + gate),
                                               in1=tile(x, n), op0=ALU.mult, op1=ALU.add).then_inc(x_upd, 1)
                        if per == 2 and start_at is not None:
                            for s in range(2):
                                modulation(q + start_at, j + s)
                        add(n, upd0 + KT)

            def mlp(layer, a, gate, upd0):
                base = layer * LAYER_QUADS + Q_MLP
                for half in range(2):
                    with dve.Fori(0, 4) as q:
                        for j in range(4):
                            n = q * 4 + (32 * layer + 16 * half + j)
                            dve.wait_ge(ff_r, n + 1)
                            V.tensor_tensor(scr[j % 2][:, :], scr[j % 2][:, :], scr[j % 2][:, :], ALU.mult).then_inc(ff_sq, 1)
                            if layer == 0:
                                modulation(q + 8 + 8 * half, j)
                            dve.wait_ge(ff_hi, n + 1)
                            V.tensor_tensor(tile(a[1], q * 4 + j), scr[j % 2][:, :], tile(a[0], q * 4 + j).bitcast(F32),
                                            ALU.subtract).then_inc(ff_lo, 1)
                    residual(4, base + 8 * half + 4, 2, gate, upd0 + KT * half,
                             12 if layer == 0 and half == 0 else None)

            dve.wait_ge(mod_set, 8)
            add_bias(16, 48)
            gains(1, C_N2, SC2)
            residual(2, Q_OUT, 1, G1, 0, None)
            norm(1, h1, KT, SH2)
            mlp(0, a0, G2, KT)
            dve.wait_ge(mod_set, 20)
            add_bias(48, 96)
            gains(2, C_N1 + 8, 48 + SC1)
            gains(3, C_N2 + 8, 48 + SC2)
            dve.wait_ge(f_w, 1)
            V.tensor_tensor(wfs[1][:, :], wf[:, :], wfs[0][:, :].bitcast(F32), ALU.subtract).then_inc(f_wl, 1)
            norm(2, h2, 2 * KT, 48 + SH1)
            dve.wait_ge(f_pe, 1)
            link(V.memset(acc[:, :], 1.0))
            dve.wait_ge(ac, 1)
            link(V.tensor_scalar(scr[0][:, :], ps[0][:, :], par[:, C_BF:C_BF + 1], 0.0, ALU.add, ALU.min))
            dve.wait_ge(f_ln, 1)
            link(V.tensor_tensor(scr[1][:, :], sqb[:, :], scr[0][:, :], ALU.subtract))
            V.tensor_tensor_scan(out=acc[:, :], data0=acc[:, :], data1=scr[1][:, :], initial=0.0,
                                 op0=ALU.mult, op1=ALU.add).then_inc(f_out, 1)
            def sums(g, w):
                for i in range(2):
                    dve.wait_ge(fx_q, 4 * g + 2 * w + i + 1)
                    V.tensor_reduce(out=ssq[:, 16 * w + 8 * i:16 * w + 8 * i + 8],
                                    in_=sqb[:, :].rearrange("p (a d) -> p a d", d=DH), axis=AX.X,
                                    op=ALU.add).then_inc(fss, 1)
                dve.wait_ge(fss, 4 * g + 2 * w + 2)
                V.tensor_scalar(ssq[:, 16 * w:16 * w + 16], ssq[:, 16 * w:16 * w + 16], 1.0 / DH, EPS,
                                ALU.mult, ALU.add).then_inc(f_var, 1)

            def normed(g, w):
                dve.wait_ge(f_rst, 2 * g + w + 1)
                for i in range(2):
                    v = qkt[w][:, 2 * i:2 * i + 2, :].rearrange("p t (a d) -> p (t a) d", d=DH)
                    V.tensor_tensor(v, v, rst[:, 16 * w + 8 * i:16 * w + 8 * i + 8].unsqueeze(2).broadcast_to([P, 8, DH]),
                                    ALU.mult).then_inc(f_nrm, 1)

            def scored(c):
                dve.wait_ge(s_pe, c + 1)
                if c >= 2:
                    dve.wait_ge(s_p, c - 1)

            def biased(s, u):
                a, i = divmod(u, TT)
                n, c = P * (i + 1), UNITS * s + u
                V.tensor_tensor_reduce(out=scr[u % 2][:, 0:n], in0=ps[bank_of(s, u, 0)][:, 0:n],
                                       in1=fb[:, FH * (s % 2) + a, 0:n], scale=-1.0, scalar=3e38,
                                       op0=ALU.add, op1=ALU.min, accum_out=small[:, c:c + 1]).then_inc(s_ns, 1)

            def turned(s, u):
                n, c = P * (u % TT + 1), UNITS * s + u
                dve.wait_ge(s_tr, c + 1)
                if c >= 2:
                    dve.wait_ge(s_pv, c - 1)
                V.tensor_copy(pT[:, u % 2, 0:n], ps[bank_of(s, u, 1)][:, 0:n]).then_inc(s_pt, 1)

            def head_out(s, a):
                c = UNITS * s + TT * a
                dve.wait_ge(s_pv, c + TT)
                V.reciprocal(rst[:, 32 + 4 * a:36 + 4 * a], den[:, c:c + TT]).then_inc(s_rd, 1)
                dve.wait_ge(s_rd, FH * s + a + 1)
                if s and a == 0:
                    dve.wait_ge(ot_tr, 2 * s)
                V.tensor_tensor(ot[:, :, DH * a:DH * a + DH],
                                ps[2][:, 0:TT * DH].rearrange("p (t d) -> p t d", d=DH),
                                rst[:, 32 + 4 * a:36 + 4 * a].unsqueeze(2).broadcast_to([P, TT, DH]),
                                ALU.mult).then_inc(s_o, 1)

            def gated(s):
                for f in range(2):
                    dve.wait_ge(ot_tr, 2 * s + f + 1)
                    dve.wait_ge(fx_g, 2 * s + 2)
                    V.tensor_tensor((acc, sqb)[f][:, :], ps[2 + f][:, :], gs[:, f, :], ALU.mult).then_inc(fy_t, 1)

            def y_lower(s):
                for f in range(2):
                    half_y(2 * s + f, (acc, sqb)[f], fy_hi, fy_lo, y1)

            for w in range(2):
                sums(0, w)
                normed(0, w)
            for s in range(GROUPS):
                dve.wait_ge(f_bc[s % 2], 16 * (s // 2 + 1))
                scored(UNITS * s)
                V.memset(dots[:, 0:1], 0.0)
                biased(s, 0)
                for u in range(UNITS):
                    if u + 1 < UNITS:
                        scored(UNITS * s + u + 1)
                    turned(s, u)
                    if u + 1 < UNITS:
                        biased(s, u + 1)
                    if s and u == 0:
                        gated(s - 1)
                    if s and u == 1:
                        y_lower(s - 1)
                    if u % TT == 1 and u > TT:
                        head_out(s, u // TT - 1)
                    if s + 1 < GROUPS:
                        for w in range(2):
                            if u == 7 + 4 * w:
                                sums(s + 1, w)
                            if u == 9 + 4 * w:
                                normed(s + 1, w)
                head_out(s, FH - 1)
            gated(GROUPS - 1)
            y_lower(GROUPS - 1)
            dve.wait_ge(fy_lo, KT)
            residual(2, LAYER_QUADS + Q_OUT, 1, 48 + G1, 3 * KT, None)
            norm(3, h3, 3 * KT, 48 + SH2)
            mlp(1, a1, 48 + G2, 4 * KT)
            root_of_x(4)
            for k in range(KT):
                V.scalar_tensor_tensor(out=x[:, k, :], in0=x[:, k, :], scalar=par[:, C_FIN + k:C_FIN + k + 1],
                                       in1=ps[7][:, :], op0=ALU.mult, op1=ALU.mult).then_inc(out_t_ready, 1)


_INS = ("x_t", "c_row", "stream", "mod_rows", "w_forget", "params")


def _laid_out(i):
    def feature_block(w, n):
        return w[:, P * n:P * n + P].reshape(KT, P, P).transpose(1, 0, 2).reshape(P, D)

    def token_blocks(w, c0):
        part = w[:, c0:c0 + GW].reshape(2, 4, P, GW).transpose(0, 2, 1, 3)
        return list(part.reshape(2, P, D))

    hg_in, fox_in = i["hg_w_in"][0], i["fox_w_in"][0]
    blocks = []
    for layer in range(2):
        def gate_blocks(g):
            w = (hg_in, fox_in)[layer]
            return [feature_block(w, 24 + 2 * g + j) for j in range(2)]

        for g in range(GROUPS):
            if g:
                blocks += gate_blocks(g - 1)
            if layer == 0:
                for part in (0, 1):
                    blocks += [feature_block(hg_in, 8 * part + 2 * g + j) for j in range(2)]
                blocks += token_blocks(hg_in, 2 * D + GW * g)
            else:
                for part in range(3):
                    blocks += token_blocks(fox_in, D * part + GW * g)
        blocks += gate_blocks(GROUPS - 1)
        w_out = i["hg_w_out" if layer == 0 else "fox_w_out"][0]
        blocks += [feature_block(w_out, n) for n in range(KT)]
        w1, w2 = i["mlp_w1"][layer], i["mlp_w2"][layer]
        for half in range(2):
            blocks += [feature_block(w1, HALF * half + n) for n in range(HALF)]
            for n in range(KT):
                for s in range(2):
                    k0 = D * (2 * half + s)
                    blocks.append(feature_block(w2[k0:k0 + D], n))
    stream = np.stack(blocks)
    mod_rows = np.ascontiguousarray(i["w_mod"].transpose(0, 2, 1)).reshape(2 * 48, P, D)
    gate = np.zeros((D, P), np.float32)
    gate[:, 0:HEADS] = fox_in[:, 4 * D:]

    def columns(v):
        return v.reshape(-1, P).T

    bias = np.zeros((P, 1), np.float32)
    bias[0:HEADS, 0] = i["fox_b_f"][0]
    twice = [np.concatenate([i[n][0], i[n][0]])[:, None] for n in ("fox_qn_w", "fox_kn_w")]
    params = np.concatenate(
        [columns(i["norm1_w"].reshape(-1)), columns(i["norm2_w"].reshape(-1)), columns(i["final_w"]),
         columns(i["hg_lb"].reshape(-1)), i["hg_gn_w"][0][:, None], *twice, bias,
         columns(i["b_mod"].reshape(-1))], axis=1)
    x_t = np.ascontiguousarray(i["x"][0].T).reshape(KT, P, T).transpose(1, 0, 2)
    return {"x_t": x_t, "c_row": i["c"], "stream": stream, "mod_rows": mod_rows,
            "w_forget": feature_block(gate, 0), "params": params}


def kernel(**inputs):
    import concourse.bacc as bacc
    from concourse.bass_utils import run_bass_kernel_spmd

    laid = _laid_out({n: np.asarray(a) for n, a in inputs.items()})
    nc = bacc.Bacc("TRN2", target_bir_lowering=False, num_devices=1)
    arrays, args = {}, []
    for name in _INS:
        arrays[name] = np.ascontiguousarray(laid[name])
        args.append(nc.dram_tensor(name, arrays[name].shape, F32, kind="ExternalInput").ap())
    args.append(nc.dram_tensor("out_t", (P, KT, T), F32, kind="ExternalOutput").ap())
    build(nc, *args)
    r = run_bass_kernel_spmd(nc, [arrays], core_ids=[0])
    got = np.asarray(r.results[0]["out_t"])
    return np.ascontiguousarray(got.transpose(2, 1, 0).reshape(1, T, D))
```

```python
import numpy as np
import concourse.bass as bass
import concourse.mybir as mybir
from concourse.alu_op_type import AluOpType as ALU
from contextlib import ExitStack

F32 = mybir.dt.float32
F32R = mybir.dt.float32r
BF16 = mybir.dt.bfloat16
U8 = mybir.dt.uint8
ACT = mybir.ActivationFunctionType
AX = mybir.AxisListType

P = 128
T = 512
TT = T // P
D = 1024
KT = D // P
EPS = 1e-6
HEADS = 16
DH = 64
GROUPS = 4
GH = 2
FH = 4
GW = D // GROUPS
FF = 4 * D
HALF = FF // 2 // P

Q_IN, Q_OUT, Q_MLP = 0, 8, 10
LAYER_QUADS = 26
QUADS = 2 * LAYER_QUADS

C_N1, C_N2, C_FIN, C_LB, C_GN, C_QN, C_KN, C_BF, C_BMOD = 0, 16, 32, 40, 64, 65, 66, 67, 68
C_ALL = C_BMOD + 96
SH1, SC1, G1, SH2, SC2, G2 = (8 * i for i in range(6))

MASKED = 8
SPLITS = 10


def build(nc, x_t, c_row, stream, mod_rows, w_forget, params, out_t):
    keep = ExitStack()
    with keep:
        def sem(name):
            return keep.enter_context(nc.semaphore(name))

        def sb(name, shape, dt, ctx=keep):
            return ctx.enter_context(nc.sbuf_tensor(name, shape, dt))

        x = sb("x", [P, KT, T], F32)
        raw = sb("raw", [P, 4, D], F32)
        whi = sb("whi", [P, 4, D], F32R)
        wlo = sb("wlo", [P, 4, D], F32R)
        par = sb("par", [P, C_ALL], F32)
        mod = sb("mod", [P, 96], F32)
        gain = sb("gain", [P, 4 * KT], F32)
        small = sb("small", [P, 64], F32)
        dots = sb("dots", [P, 4], F32)
        qkw = sb("qkw", [P, 1], F32)
        ident = sb("ident", [P, P], F32)
        identb = sb("identb", [P, P], BF16)
        causal = sb("causal", [P, P], BF16)
        mhalf = sb("mhalf", [P, 32], F32)
        ssq = sb("ssq", [P, 64], F32)
        rst = sb("rst", [P, 64], F32)
        den = sb("den", [P, 64], F32)
        meand = sb("meand", [P, 2], F32)
        scr = [sb(f"scr{i}", [P, T], F32) for i in range(2)]
        sqb = sb("sqb", [P, T], F32)
        acc = sb("acc", [P, T], F32)

        layer0 = ExitStack()
        mring = sb("mring", [P, 2, D], F32, layer0)
        cb = sb("cb", [P, D], F32, layer0)
        masks = sb("masks", [P, MASKED, P], U8, layer0)
        lbc = sb("lbc", [P, 6 * KT], F32, layer0)

        hg = ExitStack()
        h0 = [sb(n, [P, KT, T], F32R, hg) for n in ("h0hi", "h0lo")]
        head0 = ExitStack()
        modf = sb("modf", [P, 2 * KT, D], F32, head0)
        head0.close()
        hq, hk, hf = (sb(n, [P, 2 * GH, T], F32, hg) for n in ("hq", "hk", "hf"))
        hv = sb("hv", [P, TT, T], F32, hg)
        hgate = sb("hgate", [P, GH, T], F32, hg)
        adiag = sb("adiag", [P, GH, T], F32, hg)
        y0 = [sb(n, [P, KT, T], F32R, hg) for n in ("y0hi", "y0lo")]
        hg.close()
        mlp0 = ExitStack()
        a0 = [sb(n, [P, HALF, T], F32R, mlp0) for n in ("a0hi", "a0lo")]
        h1 = [sb(n, [P, KT, T], F32R, mlp0) for n in ("h1hi", "h1lo")]
        wf = sb("wf", [P, D], F32, mlp0)
        wfs = [sb(n, [P, D], F32R, mlp0) for n in ("wfhi", "wflo")]
        mlp0.close()
        layer0.close()
        fox = ExitStack()
        qkt = [sb(n, [P, TT, GW], F32, fox) for n in ("qt", "kt")]
        qkT = [sb(n, [P, 4, T], F32, fox) for n in ("qT", "kT")]
        vt = sb("vt", [P, TT, 2 * GW], F32, fox)
        gs = sb("gs", [P, 2, T], F32, fox)
        ot = sb("ot", [P, TT, GW], F32, fox)
        prob = sb("prob", [P, 2, T], F32, fox)
        pT = sb("pT", [P, 2, T], F32, fox)
        fb = sb("fb", [P, 2 * FH, T], F32, fox)
        h2 = [sb(n, [P, KT, T], F32R, fox) for n in ("h2hi", "h2lo")]
        y1 = [sb(n, [P, KT, T], F32R, fox) for n in ("y1hi", "y1lo")]
        fox.close()
        mlp1 = ExitStack()
        a1 = [sb(n, [P, HALF, T], F32R, mlp1) for n in ("a1hi", "a1lo")]
        h3 = [sb(n, [P, KT, T], F32R, mlp1) for n in ("h3hi", "h3lo")]
        mlp1.close()
        fscr = nc.dram_tensor("negf", [HEADS, T], F32).ap()

        ps = [keep.enter_context(nc.psum_tensor(f"bank{i}", [P, T], F32)) for i in range(8)]

        raw_in = [sem(f"raw_in{i}") for i in range(4)]
        w_hi, w_lo = sem("w_hi"), sem("w_lo")
        pe_blk = sem("pe_blk")
        x_in = [sem(f"x_in{i}") for i in range(2)]
        par_in, wf_in, c_in = (sem(n) for n in ("par_in", "wf_in", "c_in"))
        modf_in = [sem(f"modf_in{i}") for i in range(KT)]
        mod_in = [sem(f"mod_in{i}") for i in range(2)]
        mod_used = sem("mod_used")
        mod_set = sem("mod_set")
        consts = sem("consts")
        masked = sem("masked")
        cact = sem("cact")
        scale_mul, scale_sum = sem("scale_mul"), sem("scale_sum")
        dv = sem("dv")
        gp = sem("gp")
        ac = sem("ac")
        lb_mx, lb_ex = sem("lb_mx"), sem("lb_ex")
        x_sq, x_upd = sem("x_sq"), sem("x_upd")
        x_acc = sem("x_acc")
        n_sum, n_var, n_rst, n_bc = (sem(n) for n in ("n_sum", "n_var", "n_rst", "n_bc"))
        h_t, h_hi, h_lo = (sem(n) for n in ("h_t", "h_hi", "h_lo"))
        ev_q, ev_f, ev_v, ev_g = (sem(n) for n in ("ev_q", "ev_f", "ev_v", "ev_g"))
        kf = sem("kf")
        lvl, sel, qup, kup, kread = (sem(n) for n in ("lvl", "sel", "qup", "kup", "kread"))
        off, o_pe, o_ev = (sem(n) for n in ("off", "o_pe", "o_ev"))
        g_sum, g_var, g_rst, g_bc = (sem(n) for n in ("g_sum", "g_var", "g_rst", "g_bc"))
        hgo = sem("hgo")
        y_t, y_hi, y_lo = (sem(n) for n in ("y_t", "y_hi", "y_lo"))
        ff_r, ff_sq, ff_hi, ff_lo = (sem(n) for n in ("ff_r", "ff_sq", "ff_hi", "ff_lo"))
        f_w, f_wl, f_pe, f_ln, f_out, f_dram = (
            sem(n) for n in ("f_w", "f_wl", "f_pe", "f_ln", "f_out", "f_dram"))
        f_bc = [sem(f"f_bc{i}") for i in range(2)]
        fx_q, fx_v, fx_g = (sem(n) for n in ("fx_q", "fx_v", "fx_g"))
        fss = sem("fss")
        f_var, f_rst, f_nrm, f_tr, f_te = (sem(n) for n in ("f_var", "f_rst", "f_nrm", "f_tr", "f_te"))
        s_pe, s_ns, s_p, s_tr, s_pt, s_pv, s_rd, s_o = (
            sem(n) for n in ("s_pe", "s_ns", "s_p", "s_tr", "s_pt", "s_pv", "s_rd", "s_o"))
        ot_tr = sem("ot_tr")
        fy_t, fy_hi, fy_lo = (sem(n) for n in ("fy_t", "fy_hi", "fy_lo"))
        out_t_ready, out_done = sem("out_t_ready"), sem("out_done")

        SHARED = 3
        NORM_SQ = [1, 2, 4, 5, 7]
        UPD = [0, KT, 3 * KT, 4 * KT]
        NORM_BANKS = [ps[2:4]] + [ps[6:8]] * 4
        UNITS = FH * TT
        full = [[i] for i in range(10)] + [[10, 11], [12, 13], [14, 15]]
        HALVES = [full] * (GROUPS - 1) + [[[0], [1], [2], [3]] + [[]] * 9]
        ENDS = [[[i // 2 for i in slot if i % 2] for slot in step] for step in HALVES]
        FHALVES = [[[u] for u in range(UNITS)]] * (GROUPS - 1) + [[[0], [1], [2], [], [3]] + [[]] * (UNITS - 5)]
        FENDS = [[[i // 2 for i in slot if i % 2] for slot in step] for step in FHALVES]
        TURNS = {12: (0, 0), 13: (0, 1), 15: (1, 0)}
        TURN_LAST = 2
        TURNED = 7
        EARLY = KT - KT // GROUPS
        HPIECES = [0, 0, 0, 0, 2, 2, 2, 2, 2, 2, 4, 4, 4]
        FPIECES = [0, 0, 0, 2, 0, 2, 1, 2, 1, 1, 1, 1, 1, 1, 1, 2]
        V, S, G, PE = nc.vector, nc.scalar, nc.gpsimd, nc.tensor

        def tile(t, i):
            return t[:, bass.ds(i, 1), :].rearrange("p o n -> p (o n)")

        def col(t, i):
            return t[:, bass.ds(i, 1)]

        def cols(t, i):
            return t[:, P * i:P * (i + 1)]

        def second_halves(t, m):
            return t.rearrange("p (b h m) -> p b h m", h=2, m=m)[:, :, 1, :]

        def ended(s, slot, ends):
            s_, slot = (s, slot - 1) if slot else (s - 1, len(ends[0]) - 1)
            return [(s_, b) for b in ends[s_][slot]] if s_ >= 0 else []

        def bank_of(s, u, what):
            return 3 if s == GROUPS - 1 and what == 0 and u % 2 and u >= TURNED else what

        block = keep.enter_context(nc.Block())

        @block.sync
        def _(sp):
            sp.dma_start(cb[:, :], c_row.partition_broadcast(P)).then_inc(c_in, 16)
            sp.dma_start(par[:, :], params).then_inc(par_in, 16)
            for i in range(2):
                sp.dma_start(x[:, 4 * i:4 * i + 4, :], x_t[:, 4 * i:4 * i + 4, :]).then_inc(x_in[i], 16)
            def first_rows(k):
                rows = mod_rows[0:2 * KT].rearrange("(h m) p k -> p h m k", h=2)
                sp.dma_start(modf[:, :, :].rearrange("p (h m) k -> p h m k", h=2)[:, :, k, :],
                             rows[:, :, k, :]).then_inc(modf_in[k], 16)

            def weight(quad, j):
                sp.dma_start(raw[:, j, :], stream[bass.ds(quad * 4 + j, 1)].rearrange("b p n -> (b p) n")
                             ).then_inc(raw_in[j], 16)

            def modulation(m, s):
                sp.wait_ge(mod_used, m - 1)
                sp.dma_start(mring[:, s, :], mod_rows[bass.ds(m + 16, 1)].rearrange("b p n -> (b p) n")
                             ).then_inc(mod_in[s], 16)

            first_rows(0)
            first_rows(1)
            for j in range(4):
                weight(0, j)
            for k in range(2, KT):
                first_rows(k)
            for j in range(4):
                sp.wait_ge(w_lo, j + 1)
                weight(1, j)
                if j < 2:
                    sp.dma_start(mring[:, j, :], mod_rows[16 + j]).then_inc(mod_in[j], 16)
                else:
                    modulation(j, j % 2)

            def both(first, end, ahead):
                with sp.Fori(first, end) as q:
                    for j in range(4):
                        sp.wait_ge(w_lo, (q - 1) * 4 + j + 1)
                        weight(q, j)
                        modulation((q - ahead) * 4 + j, j % 2)

            def alone(first, end):
                with sp.Fori(first, end) as q:
                    for j in range(4):
                        sp.wait_ge(w_lo, (q - 1) * 4 + j + 1)
                        weight(q, j)

            both(2, 9, 1)
            alone(9, 11)
            both(11, 23, 3)
            sp.dma_start(wf[:, :], w_forget).then_inc(wf_in, 16)
            alone(23, QUADS)
            for k in range(KT):
                sp.wait_ge(out_t_ready, k + 1)
                sp.dma_start(out_t[:, k, :], x[:, k, :]).then_inc(out_done, 16)
            sp.wait_ge(out_done, 16 * KT)

        @block.scalar
        def _(act):
            def hi_ahead(quad, j):
                act.wait_ge(pe_blk, quad * 4 + j + 1)
                act.wait_ge(raw_in[j], quad * 16 + 32)
                S.activation(whi[:, j, :], raw[:, j, :], ACT.Copy).then_inc(w_hi, 1)

            def norm(n, h, shift, first=False):
                for k in range(KT):
                    act.wait_ge(h_t, n * KT + k + 1)
                    S.activation(h[0][:, k, :], scr[k % 2][:, :], ACT.Identity,
                                 bias=mod[:, shift + k:shift + k + 1]).then_inc(h_hi, 1)

            act.wait_ge(c_in, 16)
            S.activation(cb[:, :], cb[:, :], ACT.Silu).then_inc(cact, 1)
            act.wait_ge(lb_mx, 1)
            S.activation(lbc[:, 24:48], lbc[:, 0:24], ACT.Exp).then_inc(lb_ex, 1)
            for k in range(KT):
                if k % 4 == 0:
                    act.wait_ge(x_in[k // 4], 16)
                if k >= 2:
                    act.wait_ge(x_acc, k - 1)
                S.activation((sqb, scr[0])[k % 2][:, :], x[:, k, :], ACT.Square).then_inc(x_sq, 1)
            for j in range(4):
                act.wait_ge(raw_in[j], 16)
                S.activation(whi[:, j, :], raw[:, j, :], ACT.Copy).then_inc(w_hi, 1)
            for k in range(KT):
                act.wait_ge(h_t, k + 1)
                S.activation(h0[0][:, k, :], scr[k % 2][:, :], ACT.Identity,
                             bias=mod[:, SH1 + k:SH1 + k + 1]).then_inc(h_hi, 1)
                if SHARED <= k + 1 < KT:
                    m = KT + k + 1
                    act.wait_ge(scale_mul, k + 2 - SHARED)
                    S.activation(modf[:, m, :], modf[:, m, :], ACT.Copy,
                                 accum_out=mod[:, m:m + 1]).then_inc(scale_sum, 1)

            def hg_dense(s, b):
                n = 6 + 8 * s + b
                g, j = s + 1, b % 2
                at = 2 * (g % 2) + j
                act.wait_ge(pe_blk, n + 1)
                if s < 0 and b < 6:
                    hi_ahead(n // 4, n % 4)
                if b < 2:
                    S.activation(hgate[:, j, :], ps[6 + j][:, :], ACT.Silu).then_inc(ev_g, 1)
                elif b < 4:
                    if g >= 2:
                        act.wait_ge(y_t, 2 * (g - 2) + 2)
                    S.activation(hq[:, at, :], ps[4 + j][:, :], ACT.Silu).then_inc(ev_q, 1)
                elif b < 6:
                    S.activation(hf[:, at, :], ps[6 + j][:, :], ACT.Sigmoid)
                    S.activation(hk[:, at, :], ps[6 + j][:, :], ACT.Sigmoid, scale=-1.0).then_inc(ev_f, 1)
                elif b == 7:
                    for i in range(2):
                        S.activation(hv[:, 2 * i:2 * i + 2, GW * (g % 2):GW * (g % 2) + GW],
                                     ps[(4 if g else 2) + i][:, :].rearrange("p (t v) -> p t v", v=GW), ACT.Copy).then_inc(ev_v, 1)
                if s >= 0 or b >= 6:
                    hi_ahead(n // 4, n % 4)

            def hg_core(s, slot):
                p0 = 2 * (s % 2)
                if slot == 9:
                    for j in range(GH):
                        act.wait_ge(lvl, 20 * s + 18 + 2)
                        S.activation(hf[:, p0 + j, :], ps[j][:, :], ACT.Copy)
                        S.activation(hk[:, p0 + j, 256:512], ps[2][:, 256 * j:256 * j + 256], ACT.Copy).then_inc(off, 1)
                elif slot == 10:
                    for j in range(GH):
                        act.wait_ge(o_pe, 2 * s + j + 1)
                        S.activation(hk[:, p0 + j, :], ps[3 - j][:, :], ACT.Square)
                        S.activation(hq[:, p0 + j, :], ps[3 - j][:, :], ACT.Copy).then_inc(o_ev, 1)
                elif slot == 12:
                    for j in range(GH):
                        act.wait_ge(y_t, 2 * s + j + 1)
                        S.activation(y0[0][:, 2 * s + j, :], scr[j][:, :], ACT.Copy).then_inc(y_hi, 1)

            for b in range(2, 8):
                hg_dense(-1, b)
            for s in range(GROUPS):
                for slot in range(len(ENDS[s])):
                    hg_core(s, slot)
                    for s_, b in ended(s, slot, ENDS):
                        hg_dense(s_, b)

            def residual(quads, q0, per, sq0, first):
                def body(q, last):
                    for j in range(4):
                        if not last and j < 3:
                            hi_ahead(q0 + q, j)
                        if j % per == per - 1:
                            n = q * (4 // per) + j // per
                            act.wait_ge(x_upd, sq0 + n + 1)
                            act.wait_ge(x_acc, sq0 + n + KT)
                            S.activation(sqb[:, :], tile(x, n), ACT.Square).then_inc(x_sq, 1)
                        if not last and j == 3:
                            hi_ahead(q0 + q, j)
                n_loop = quads - (1 if first else 0)
                with act.Fori(0, n_loop) as q:
                    body(q, False)
                if first:
                    body(quads - 1, True)

            def mlp(layer, a, sq0):
                base = layer * LAYER_QUADS + Q_MLP
                for half in range(2):
                    with act.Fori(0, 4) as q:
                        for j in range(4):
                            act.wait_ge(pe_blk, (q + base + 8 * half) * 4 + j + 1)
                            ff_n = (q + 4 * half) * 4 + j + 32 * layer
                            if layer or half or j >= 2:
                                act.wait_ge(ff_lo, ff_n - 1)
                            S.activation(scr[j % 2][:, :], ps[j][:, :], ACT.Relu).then_inc(ff_r, 1)
                            hi_ahead(q + base + 8 * half, j)
                            act.wait_ge(ff_sq, ff_n + 1)
                            S.activation(tile(a[0], q * 4 + j), scr[j % 2][:, :], ACT.Copy).then_inc(ff_hi, 1)
                    if layer == 0 and half:
                        act.wait_ge(wf_in, 16)
                        S.activation(wfs[0][:, :], wf[:, :], ACT.Copy).then_inc(f_w, 1)
                    residual(4, base + 8 * half + 4, 2, sq0 + KT * half, layer == 1 and half == 1)

            residual(2, Q_OUT, 1, 0, False)
            norm(1, h1, SH2)
            mlp(0, a0, KT)
            norm(2, h2, 48 + SH1)
            act.wait_ge(f_pe, 1)
            S.activation(gs[:, 0, :], ps[0][:, :], ACT.Abs, bias=par[:, C_BF:C_BF + 1]).then_inc(ac, 1)
            act.wait_ge(ac, 1)
            S.activation(gs[:, 0, :], gs[:, 0, :], ACT.Exp, scale=-1.0).then_inc(ac, 1)
            act.wait_ge(ac, 2)
            S.activation(gs[:, 0, :], gs[:, 0, :], ACT.Ln, bias=1.0).then_inc(f_ln, 1)

            L = LAYER_QUADS

            def forget(g):
                act.dma_start(fb[:, FH * (g % 2):FH * (g % 2) + FH, :],
                              fscr[FH * g:FH * g + FH, :].partition_broadcast(P)).then_inc(f_bc[g % 2], 16)

            def fox_dense(s, b):
                n = 4 * L + 6 + 8 * s + b
                g = s + 1
                act.wait_ge(pe_blk, n + 1)
                if b < 2:
                    S.activation(gs[:, b, :], ps[6 + b][:, :], ACT.Sigmoid).then_inc(fx_g, 1)
                elif b in (3, 5):
                    w = (b - 3) // 2
                    for i in range(2):
                        c = 4 * g + 2 * w + i
                        if c > 1:
                            act.wait_ge(fss, c - 1)
                        if g:
                            act.wait_ge(f_tr, 4 * (g - 1) + 2 * w + 2)
                        S.activation((sqb, acc)[i][:, :], ps[4 + 2 * w + i][:, :], ACT.Square)
                        S.activation(qkt[w][:, 2 * i:2 * i + 2, :],
                                     ps[4 + 2 * w + i][:, :].rearrange("p (t v) -> p t v", v=GW),
                                     ACT.Copy).then_inc(fx_q, 1)
                elif b == 7:
                    for i in range(2):
                        S.activation(vt[:, 2 * i:2 * i + 2, GW * (g % 2):GW * (g % 2) + GW],
                                     ps[4 + i][:, :].rearrange("p (t v) -> p t v", v=GW), ACT.Copy).then_inc(fx_v, 1)
                hi_ahead(n // 4, n % 4)

            def turned_out(g, w, f):
                scale = (qkw[:, 0:1], par[:, C_KN:C_KN + 1])[w]
                act.wait_ge(f_tr, 4 * g + 2 * w + f + 1)
                S.activation(qkT[w][:, 2 * (g % 2) + f, :], ps[3][:, :], ACT.Copy, scale=scale).then_inc(f_te, 1)

            def y_upper(s):
                for f in range(2):
                    act.wait_ge(fy_t, 2 * s + f + 1)
                    S.activation(y1[0][:, 2 * s + f, :], (acc, sqb)[f][:, :], ACT.Copy).then_inc(fy_hi, 1)

            fox_dense(-1, 2)
            fox_dense(-1, 3)
            act.wait_ge(f_out, 1)
            act.dma_start(fscr, gs[0:HEADS, 1, :]).then_inc(f_dram, 16)
            fox_dense(-1, 4)
            act.wait_ge(f_dram, 16)
            forget(0)
            fox_dense(-1, 5)
            fox_dense(-1, 6)
            turned_out(0, 0, 0)
            fox_dense(-1, 7)
            turned_out(0, 0, 1)
            turned_out(0, 1, 0)
            for s in range(GROUPS):
                if s + 1 < GROUPS:
                    if s >= 1:
                        act.wait_ge(s_ns, UNITS * s)
                    forget(s + 1)
                for u in range(UNITS):
                    n, c = P * (u % TT + 1), UNITS * s + u
                    if s and u == 0:
                        turned_out(s, *TURNS[UNITS - 1])
                    act.wait_ge(s_ns, c + 1)
                    if c >= 2:
                        act.wait_ge(s_tr, c - 1)
                    S.activation(prob[:, u % 2, 0:n], scr[u % 2][:, 0:n], ACT.Exp, scale=-1.0,
                                 bias=small[:, c:c + 1], accum_out=den[:, c:c + 1]).then_inc(s_p, 1)
                    if s and u == 1:
                        y_upper(s - 1)
                    if u == TURN_LAST + 1:
                        turned_out(s, 1, 1)
                    if s + 1 < GROUPS and u - 1 in TURNS:
                        turned_out(s + 1, *TURNS[u - 1])
                    for s_, b in ended(s, u, FENDS):
                        fox_dense(s_, b)
            y_upper(GROUPS - 1)
            residual(2, L + Q_OUT, 1, 3 * KT, False)
            norm(3, h3, 48 + SH2)
            mlp(1, a1, 4 * KT)

        @block.gpsimd
        def _(pool):
            G.memset(ident[:, :], 0.0).then_inc(gp, 1)
            G.memset(mhalf[:, :], -0.5).then_inc(gp, 1)
            G.memset(meand[:, 0:1], 1.0 / D)
            G.memset(meand[:, 1:2], 1.0 / P)
            pool.wait_ge(gp, 1)
            G.affine_select(out=ident[:, :], in_=ident[:, :], compare_op=ALU.not_equal, fill=1.0,
                            base=0, pattern=[[-1, P]], channel_multiplier=1).then_inc(gp, 1)
            pool.wait_ge(gp, 3)
            G.tensor_copy(identb[:, :], ident[:, :]).then_inc(gp, 1)
            G.memset(causal[:, :], 0.0).then_inc(gp, 1)
            pool.wait_ge(gp, 5)
            G.affine_select(out=causal[:, :], in_=causal[:, :], compare_op=ALU.is_ge, fill=-3e38,
                            base=0, pattern=[[-1, P]], channel_multiplier=1).then_inc(gp, 1)
            pool.wait_ge(gp, 6)
            G.memset(dots[:, 0:1], 0.0).then_inc(consts, 1)
            n = 6
            for lv in range(MASKED):
                pool.wait_ge(gp, n)
                if lv:
                    m = 1 << (lv - 1)
                    nb = P // (2 * m)
                    v = scr[1][:, 0:P].rearrange("p (b h m) -> p b h m", h=2, m=m)
                    G.memset(v[:, :, 0, :], 0.0)
                    G.memset(v[:, :, 1, :], 1.0).then_inc(gp, 1)
                    pool.wait_ge(gp, n + 1)
                    G.affine_select(out=v[:, :, 1, :], in_=v[:, :, 1, :], compare_op=ALU.is_ge, fill=0.0,
                                    base=0, pattern=[[-2 * m, nb], [0, m]], channel_multiplier=1).then_inc(gp, 1)
                    pool.wait_ge(gp, n + 2)
                    G.affine_select(out=v[:, :, 1, :], in_=v[:, :, 1, :], compare_op=ALU.is_gt, fill=0.0,
                                    base=m, pattern=[[2 * m, nb], [0, m]], channel_multiplier=-1).then_inc(gp, 1)
                    pool.wait_ge(gp, n + 3)
                    G.tensor_copy(masks[:, lv, :], scr[1][:, 0:P]).then_inc(gp, 1)
                    n += 4
            pool.wait_ge(gp, n)
            G.memset(scr[1][:, 0:1], 0.0).then_inc(masked, 1)

            def lo(quad_plus, j):
                pool.wait_ge(w_hi, quad_plus * 4 + j + 1)
                G.tensor_tensor(wlo[:, j, :], raw[:, j, :], whi[:, j, :].bitcast(F32), ALU.subtract).then_inc(w_lo, 1)

            def root(ready, ready_at, n, done, at=0):
                pool.wait_ge(ready, ready_at)
                G.tensor_tensor(rst[:, at:at + n], ssq[:, at:at + n], mhalf[:, 0:n], ALU.pow).then_inc(done, 1)

            root(n_var, 1, TT, n_rst)
            for j in range(4):
                lo(0, j)
            pool.wait_ge(cact, 1)
            for k in range(SHARED, KT):
                pool.wait_ge(modf_in[k], 16)
                G.tensor_tensor(modf[:, KT + k, :], modf[:, KT + k, :], cb[:, :], ALU.mult).then_inc(scale_mul, 1)

            def lo_ahead(n):
                lo(n // 4 + 1, n % 4)

            for b in range(6):
                lo_ahead(b)
            for s in range(GROUPS):
                p0 = 2 * (s % 2)
                for slot in range(len(ENDS[s])):
                    if 1 <= slot < SPLITS - 1:
                        m = 1 << (slot - 1)
                        shape = [P, T // (2 * m), m]
                        for j in range(GH):
                            kv = hk[:, p0 + j, :].rearrange("p (b h m) -> p b h m", h=2, m=m)
                            tv = hf[:, p0 + j, :].rearrange("p (b h m) -> p b h m", h=2, m=m)
                            pool.wait_ge(lvl, 20 * s + 2 * slot + j + 1)
                            last = slot == SPLITS - 2
                            G.tensor_tensor(kv[:, :, 0, :], kv[:, :, 0, :], tv[:, :, 1, 0:1].broadcast_to(shape),
                                            ALU.mult).then_inc(kup if last else kread, 1)
                            if not last:
                                pool.wait_ge(kread, 14 * s + 2 * (slot - 1) + j + 1)
                                pool.wait_ge(qup, 18 * s + 2 * slot + j + 1)
                                G.tensor_tensor(tv[:, :, 0, 0], tv[:, :, 0, 0], tv[:, :, 1, 0],
                                                ALU.mult).then_inc(kup, 1)
                    if slot == 11:
                        root(g_var, s + 1, 4 * GH, g_rst)
                    for s_, b in ended(s, slot, ENDS):
                        lo_ahead(6 + 8 * s_ + b)
            def lo_quads(first, end, n):
                with pool.Fori(first, end - 1) as q:
                    for j in range(4):
                        lo(q, j)
                for j in range(4):
                    if j == 3:
                        root(n_var, n, TT, n_rst)
                    lo(end - 1, j)

            lo_quads(Q_OUT + 1, Q_OUT + 3, 2)
            lo_quads(Q_MLP + 1, LAYER_QUADS + 1, 3)
            L = LAYER_QUADS
            for s in range(-1, GROUPS):
                for b in range(2 if s < 0 else 0, 2 if s == GROUPS - 1 else 8):
                    if b in (3, 5):
                        w = (b - 3) // 2
                        root(f_var, 2 * (s + 1) + w + 1, 16, f_rst, 16 * w)
                    lo_ahead(4 * L + 6 + 8 * s + b)
            lo_quads(L + Q_OUT + 1, L + Q_OUT + 3, 4)
            with pool.Fori(L + Q_MLP + 1, QUADS) as q:
                for j in range(4):
                    lo(q, j)
            root(n_var, 5, TT, n_rst)

        @block.tensor
        def _(pe):
            def split(quad, j):
                pe.wait_ge(w_hi, quad * 4 + j + 1)
                pe.wait_ge(w_lo, quad * 4 + j + 1)

            def product(out, w, k, hh, first, last):
                wh, wl = whi[:, w, P * k:P * k + P], wlo[:, w, P * k:P * k + P]
                PE.matmul(out, wh, hh[0], start=first, stop=False)
                PE.matmul(out, wh, hh[1], start=False, stop=False)
                return PE.matmul(out, wl, hh[0], start=False, stop=last)

            def feature_block(quad, j, bank, h, k0=0, first=True, last=True):
                split(quad, j)
                for k in range(KT):
                    mm = product(ps[bank][:, :], j, k, [h[0][:, k0 + k, :], h[1][:, k0 + k, :]],
                                 first and k == 0, last and k == KT - 1)
                mm.then_inc(pe_blk, 1)

            def norm(n):
                sums, spread = NORM_BANKS[n]
                pe.wait_ge(x_acc, KT * NORM_SQ[n] - 1)
                for t in range(TT):
                    PE.matmul(sums[:, t:t + 1], cols(acc, t), meand[:, 0:1], start=t == 0, stop=False,
                              skip_group_check=True)
                pe.wait_ge(x_sq, KT * NORM_SQ[n])
                last = scr[0] if n == 0 else sqb
                for t in range(TT):
                    mm = PE.matmul(sums[:, t:t + 1], cols(last, t), meand[:, 0:1], start=False, stop=True,
                                   skip_group_check=True)
                mm.then_inc(n_sum, 1)
                pe.wait_ge(n_rst, n + 1)
                for t in range(TT):
                    mm = PE.matmul(cols(spread, t), rst[:, t:t + 1].broadcast_to([P, P]), ident[:, :],
                                   start=True, stop=True)
                mm.then_inc(n_bc, 1)

            pe.wait_ge(consts, 1)
            norm(0)

            def half_feature(n, half, bank, h):
                if half == 0:
                    split(n // 4, n % 4)
                for k in range(4 * half, 4 * half + 4):
                    mm = product(ps[bank][:, :], n % 4, k, [h[0][:, k, :], h[1][:, k, :]], k == 0, k == KT - 1)
                if half:
                    mm.then_inc(pe_blk, 1)

            def quarter_token(n, quarter, bank, h):
                j = n % 4
                if quarter % 2 == 0:
                    split(n // 4, j)
                for k in (2 * quarter, 2 * quarter + 1):
                    w0 = slice(GW * (k % 4), GW * (k % 4) + GW)
                    for t in range(TT):
                        o = ps[bank + t // 2][:, GW * (t % 2):GW * (t % 2) + GW]
                        hh, hl = cols(h[0][:, k, :], t), cols(h[1][:, k, :], t)
                        PE.matmul(o, hh, whi[:, j, w0], start=k == 0 and t % 2 == 0, stop=False, skip_group_check=True)
                        PE.matmul(o, hl, whi[:, j, w0], start=False, stop=False, skip_group_check=True)
                        mm = PE.matmul(o, hh, wlo[:, j, w0], start=False, stop=k == KT - 1, skip_group_check=True)
                if quarter % 2:
                    mm.then_inc(pe_blk, 1)

            def hg_half(s, i):
                b, half = i // 2, i % 2
                n, g, j = 6 + 8 * s + b, s + 1, b % 2
                if half == 0:
                    if b < 2:
                        pe.wait_ge(ev_f, 2 * s + j + 1)
                    elif b < 4 and g:
                        pe.wait_ge(ev_v, 2 * (g - 1) + 2)
                    elif b in (4, 5) and g:
                        pe.wait_ge(ev_g, 2 * s + j + 1)
                    elif b == 6 and g:
                        pe.wait_ge(ev_q, 2 * g + 2)
                if b < 6:
                    half_feature(n, half, (6, 4, 6)[b // 2] + j, h0)
                else:
                    quarter_token(n, i - 12, 4 if g else 2, h0)

            def together(jobs, h, ready):
                for k in range(KT):
                    pe.wait_ge(h_lo, ready + k + 1)
                    for quad, j, bank in jobs:
                        if k == 0:
                            split(quad, j)
                        mm = product(ps[bank][:, :], j, k, [h[0][:, k, :], h[1][:, k, :]], k == 0, k == KT - 1)
                        if k == KT - 1:
                            mm.then_inc(pe_blk, 1)

            together([(0, j, 4 + j) for j in range(4)], h0, 0)
            for i in range(12, 16):
                hg_half(-1, i)

            def hg_core(s, slot):
                p0 = 2 * (s % 2)
                for j in range(GH):
                    kk, qq = hk[:, p0 + j, :], hq[:, p0 + j, :]
                    if slot < SPLITS:
                        lv = slot
                        if lv == 0:
                            pe.wait_ge(kf, 2 * s + j + 1)
                            pe.wait_ge(ev_q, 2 * s + j + 1)
                            pe.wait_ge(y_t, 2 * s)
                        else:
                            pe.wait_ge(qup, 18 * s + 2 * (lv - 1) + j + 1)
                            if lv >= 2:
                                pe.wait_ge(kup, 16 * s + 2 * (lv - 2) + j + 1)
                            if lv == SPLITS - 1 and j == 0:
                                pe.wait_ge(ev_v, 2 * s + 2)
                            if lv <= MASKED:
                                pe.wait_ge(sel, 16 * s + 2 * (lv - 1) + j + 1)
                        if lv == 0:
                            for t in range(TT):
                                mm = PE.matmul(cols(ps[j], t), cols(kk, t), cols(qq, t), start=True, stop=True)
                        elif lv == MASKED - 1:
                            m = P // 2
                            for t in range(TT):
                                mm = PE.matmul(ps[j][0:m, P * t + m:P * t + P], kk[:, P * t:P * t + m],
                                               qq[:, P * t + m:P * t + P], start=True, stop=True)
                        elif lv < MASKED - 1:
                            m = 1 << (lv - 1)
                            for t in range(TT):
                                mm = PE.matmul(second_halves(cols(ps[j], t), m), cols(kk, t),
                                               second_halves(cols(qq, t), m), start=True, stop=True)
                        elif lv == 8:
                            PE.matmul(cols(ps[j], 0), cols(kk, 0), cols(qq, 1), start=True, stop=True)
                            mm = PE.matmul(cols(ps[j], 3), cols(kk, 2), cols(qq, 3), start=True, stop=True)
                        else:
                            PE.matmul(ps[j][:, 128:384], cols(kk, 0), qq[:, 256:512], start=True, stop=True)
                            mm = PE.matmul(ps[2][:, 256 * j:256 * j + 256], cols(kk, 1), qq[:, 256:512],
                                           start=True, stop=True)
                        mm.then_inc(lvl, 1)
                    elif slot == 10:
                        pe.wait_ge(off, 2 * s + GH)
                        o, at = ps[3 - j], p0 + j
                        v = [hv[:, t, P * at:P * at + P] for t in range(TT)]
                        f_, k_ = hf[:, at, :], hk[:, at, :]
                        parts = [(0, P, v[0], cols(adiag[:, j, :], 0)), (P, T, v[0], f_[:, 0:384]),
                                 (256, T, v[1], k_[:, 256:512]), (384, T, v[2], f_[:, 384:512])]
                        parts += [(P * t, P * t + P, v[t], cols(adiag[:, j, :], t)) for t in range(1, TT)]
                        for i, (a, b, lhs, rhs) in enumerate(parts):
                            mm = PE.matmul(o[:, a:b], lhs, rhs, start=i == 0, stop=i == len(parts) - 1,
                                           skip_group_check=True)
                        mm.then_inc(o_pe, 1)
                    elif slot == 11:
                        pe.wait_ge(o_ev, 2 * s + j + 1)
                        for t in range(TT):
                            mm = PE.matmul(ps[0][:, 4 * j + t:4 * j + t + 1], cols(kk, t), meand[:, 1:2],
                                           start=True, stop=True)
                        if j == GH - 1:
                            mm.then_inc(g_sum, 1)
                    else:
                        pe.wait_ge(g_rst, s + 1)
                        for t in range(TT):
                            root = rst[:, 4 * j + t:4 * j + t + 1]
                            mm = PE.matmul(cols(ps[1 + 2 * j], t), root.broadcast_to([P, P]), ident[:, :],
                                           start=True, stop=True)
                        mm.then_inc(g_bc, 1)

            def w_out_begin(quad, y, first, end):
                for i in range(first, end):
                    j, k = divmod(i, EARLY)
                    if k == 0:
                        split(quad, j)
                    product(ps[4 + j][:, :], j, k, [y[0][:, k, :], y[1][:, k, :]], k == 0, False)

            def w_out(quad, y, y_done, upd0):
                pe.wait_ge(*y_done)
                for j in range(4):
                    for k in range(EARLY, KT):
                        mm = product(ps[4 + j][:, :], j, k, [y[0][:, k, :], y[1][:, k, :]], False, k == KT - 1)
                    mm.then_inc(pe_blk, 1)
                for j in range(4):
                    pe.wait_ge(x_upd, upd0 + j + 1)
                    feature_block(quad + 1, j, 4 + j, y)

            done = 0
            for s in range(GROUPS):
                for slot, halves in enumerate(HALVES[s]):
                    hg_core(s, slot)
                    for i in halves:
                        hg_half(s, i)
                    if s == GROUPS - 1 and HPIECES[slot]:
                        if done == 0:
                            pe.wait_ge(y_lo, EARLY)
                            pe.wait_ge(ev_g, 2 * GROUPS)
                            pe.wait_ge(ev_v, 2 * GROUPS)
                        w_out_begin(Q_OUT, y0, done, done + HPIECES[slot])
                        done += HPIECES[slot]

            def mlp(layer, h, a, n):
                base = layer * LAYER_QUADS + Q_MLP
                for half in range(2):
                    first = 0
                    if half == 0:
                        if layer:
                            pe.wait_ge(ff_r, 32 * layer)
                        together([(base, j, j) for j in range(2)], h, KT * n)
                        for j in range(2, 4):
                            feature_block(base, j, j, h)
                        first = 1
                    with pe.Fori(first, 4) as q:
                        for j in range(4):
                            pe.wait_ge(ff_r, q * 4 + (32 * layer + 16 * half + j - 3))
                            feature_block(q + base + 8 * half, j, j, h)
                    with pe.Fori(0, 4) as q:
                        for j in range(4):
                            if j % 2 == 0:
                                pe.wait_ge(x_upd, q * 2 + (UPD[2 * layer + 1] + KT * half + j // 2 - 1))
                            if j < 2:
                                pe.wait_ge(ff_lo, 32 * layer + 16 * half + KT * (j + 1))
                            feature_block(q + base + 8 * half + 4, j, 4 + j // 2, a, k0=KT * (j % 2),
                                          first=j % 2 == 0, last=j % 2 == 1)

            w_out(Q_OUT, y0, (y_lo, KT), 0)
            norm(1)
            mlp(0, h1, a0, 1)
            norm(2)
            L = LAYER_QUADS

            def fox_half(s, i):
                b, half = i // 2, i % 2
                n, g = 4 * L + 6 + 8 * s + b, s + 1
                if half == 0:
                    if b < 2:
                        pe.wait_ge(fx_q, 4 * s + 4)
                    elif b == 2 and g:
                        pe.wait_ge(fx_v, 2 * g)
                    elif b == 4 and g:
                        pe.wait_ge(fx_g, 2 * g)
                    elif b == 6:
                        pe.wait_ge(fx_q, 4 * g + 2)
                if b < 2:
                    half_feature(n, half, 6 + b, h2)
                else:
                    quarter_token(n, (i - 4) % 4, (4, 6, 4)[(b - 2) // 2], h2)

            def turn(g, w, f):
                pe.wait_ge(f_nrm, 4 * g + 2 * w + 2)
                if g or w or f:
                    pe.wait_ge(f_te, 4 * g + 2 * w + f)
                for t in range(TT):
                    mm = PE.transpose(cols(ps[3], t), cols(qkt[w][:, t, :], f), ident[:, :])
                mm.then_inc(f_tr, 1)

            def scores(s, u):
                a, i = divmod(u, TT)
                r, f = DH * (a % 2), 2 * (s % 2) + a // 2
                c = UNITS * s + u
                if u == 0:
                    pe.wait_ge(f_te, 4 * s + 3)
                if u == TURNED:
                    pe.wait_ge(f_te, 4 * s + 4)
                if c >= 1:
                    pe.wait_ge(s_ns, c if s < GROUPS - 1 or u < TURNED else c - 1)
                n = P * (i + 1)
                o = ps[bank_of(s, u, 0)]
                PE.matmul(o[:, 0:n], qkT[0][r:r + DH, f, P * i:P * i + P], qkT[1][r:r + DH, f, 0:n],
                          start=True, stop=False, skip_group_check=True)
                PE.matmul(o[:, n - P:n], identb[:, :], causal[:, :],
                          start=False, stop=True, skip_group_check=True).then_inc(s_pe, 1)

            def transposes(s, u):
                c = UNITS * s + u
                pe.wait_ge(s_p, c + 1)
                if c >= 1:
                    pe.wait_ge(s_pt, c)
                for t in range(u % TT + 1):
                    mm = PE.transpose(cols(ps[bank_of(s, u, 1)], t), cols(prob[:, u % 2, :], t), ident[:, :])
                mm.then_inc(s_tr, 1)

            def values(s, u):
                a, i = divmod(u, TT)
                pe.wait_ge(s_pt, UNITS * s + u + 1)
                if u == 0:
                    pe.wait_ge(fx_v, 2 * s + 2)
                if i == 0:
                    pe.wait_ge(s_o, FH * s + a)
                    pe.wait_ge(fy_t, 2 * s)
                v0 = GW * (s % 2) + DH * a
                for t in range(i + 1):
                    mm = PE.matmul(ps[2][:, DH * i:DH * i + DH], cols(pT[:, u % 2, :], t),
                                   vt[:, t, v0:v0 + DH], start=t == 0, stop=t == i)
                mm.then_inc(s_pv, 1)

            def turn_o(s):
                pe.wait_ge(s_o, FH * s + FH)
                for f in range(2):
                    for t in range(TT):
                        mm = PE.transpose(cols(ps[2 + f], t), cols(ot[:, t, :], f), ident[:, :])
                    mm.then_inc(ot_tr, 1)

            pe.wait_ge(f_wl, 1)
            for kk in range(KT // 2):
                for k in (2 * kk, 2 * kk + 1):
                    pe.wait_ge(h_lo, 2 * KT + k + 1)
                    wh, wl = cols(wfs[0], k), cols(wfs[1], k)
                    PE.matmul(ps[0][:, :], wh, h2[0][:, k, :], start=k == 0, stop=False)
                    PE.matmul(ps[0][:, :], wh, h2[1][:, k, :], start=False, stop=False)
                    mm = PE.matmul(ps[0][:, :], wl, h2[0][:, k, :], start=False, stop=k == KT - 1)
                if kk == KT // 2 - 1:
                    mm.then_inc(f_pe, 1)
                fox_half(-1, 4 + kk)
            for i in range(8, 16):
                fox_half(-1, i)
                if i in (13, 15):
                    turn(0, 0, (i - 13) // 2)
            turn(0, 1, 0)
            pe.wait_ge(f_out, 1)
            done = 0
            for s in range(GROUPS):
                if s == 0:
                    scores(0, 0)
                for u in range(UNITS):
                    if u + 1 < UNITS:
                        scores(s, u + 1)
                    transposes(s, u)
                    if s + 1 < GROUPS and u in TURNS:
                        turn(s + 1, *TURNS[u])
                    for i in FHALVES[s][u]:
                        fox_half(s, i)
                    if s == GROUPS - 1 and FPIECES[u]:
                        if done == 0:
                            pe.wait_ge(fy_lo, EARLY)
                        if done <= 2 * EARLY < done + FPIECES[u]:
                            pe.wait_ge(fx_g, 2 * GROUPS)
                        w_out_begin(L + Q_OUT, y1, done, done + FPIECES[u])
                        done += FPIECES[u]
                    if s and u == 0:
                        turn_o(s - 1)
                    if u >= 1:
                        values(s, u - 1)
                    if u == TURN_LAST:
                        turn(s, 1, 1)
                if s + 1 < GROUPS:
                    scores(s + 1, 0)
                values(s, UNITS - 1)
            w_out_begin(L + Q_OUT, y1, done, done + 4)
            turn_o(GROUPS - 1)
            w_out_begin(L + Q_OUT, y1, done + 4, 4 * EARLY)
            w_out(L + Q_OUT, y1, (fy_lo, KT), UPD[2])
            norm(3)
            mlp(1, h3, a1, 3)
            norm(4)

        @block.vector
        def _(dve):
            chain = [0]

            def link(ins):
                chain[0] += 1
                ins.then_inc(dv, 1)
                dve.wait_ge(dv, chain[0])

            def eps_var(bank_cols, n, at=0):
                return V.tensor_scalar(ssq[:, at:at + n], bank_cols, EPS, None, ALU.add)

            def root_of_x(n):
                dve.wait_ge(n_sum, n + 1)
                eps_var(NORM_BANKS[n][0][:, 0:TT], TT).then_inc(n_var, 1)
                V.memset(acc[:, :], 0.0).then_inc(x_acc, 1)
                dve.wait_ge(n_bc, n + 1)

            def t_of(n, k, gain0):
                if n * KT + k >= 2:
                    dve.wait_ge(h_lo, n * KT + k - 1)
                V.scalar_tensor_tensor(out=scr[k % 2][:, :], in0=x[:, k, :], scalar=gain[:, gain0 + k:gain0 + k + 1],
                                       in1=NORM_BANKS[n][1][:, :], op0=ALU.mult, op1=ALU.mult).then_inc(h_t, 1)

            def lower(n, k, h, shift):
                dve.wait_ge(h_hi, n * KT + k + 1)
                V.scalar_tensor_tensor(out=h[1][:, k, :], in0=scr[k % 2][:, :],
                                       scalar=mod[:, shift + k:shift + k + 1],
                                       in1=h[0][:, k, :].bitcast(F32), op0=ALU.add,
                                       op1=ALU.subtract).then_inc(h_lo, 1)

            def norm(n, h, gain0, shift):
                root_of_x(n)
                t_of(n, 0, gain0)
                for k in range(KT):
                    if k + 1 < KT:
                        t_of(n, k + 1, gain0)
                    lower(n, k, h, shift)

            def modulation(mq, j):
                s = j % 2
                dve.wait_ge(mod_in[s], mq * 32 + 16 * (j // 2 + 1))
                if j == 0 and not (isinstance(mq, int) and mq == 0):
                    dve.wait_ge(mod_set, mq)
                V.tensor_tensor_reduce(out=mring[:, s, :], in0=mring[:, s, :], in1=cb[:, :], scale=1.0, scalar=0.0,
                                       op0=ALU.mult, op1=ALU.add, accum_out=dots[:, j:j + 1]).then_inc(mod_used, 1)
                if j == 3:
                    dve.wait_ge(mod_used, mq * 4 + 4)
                    V.tensor_copy(mod[:, bass.ds(mq * 4 + 16, 4)], dots[:, :]).then_inc(mod_set, 1)

            def add_bias(lo_, hi_):
                link(V.tensor_tensor(mod[:, lo_:hi_], mod[:, lo_:hi_], par[:, C_BMOD + lo_:C_BMOD + hi_], ALU.add))

            def gains(i, norm_col, scale_col):
                link(V.scalar_tensor_tensor(out=gain[:, KT * i:KT * i + KT], in0=mod[:, scale_col:scale_col + KT],
                                            scalar=1.0, in1=par[:, norm_col:norm_col + KT],
                                            op0=ALU.add, op1=ALU.mult))

            def half_y(n, t, hi_sem, lo_sem, y):
                dve.wait_ge(hi_sem, n + 1)
                V.tensor_tensor(y[1][:, n, :], t[:, :], y[0][:, n, :].bitcast(F32), ALU.subtract).then_inc(lo_sem, 1)

            dve.wait_ge(par_in, 16)
            lb = [par[:, C_LB + KT * i:C_LB + KT * i + KT] for i in range(3)]
            link(V.tensor_tensor(small[:, 0:8], lb[0], lb[1], ALU.max))
            link(V.tensor_tensor(small[:, 8:16], small[:, 0:8], lb[2], ALU.max))
            for i in range(3):
                ins = V.tensor_tensor(lbc[:, KT * i:KT * i + KT], lb[i], small[:, 8:16], ALU.subtract)
            ins.then_inc(lb_mx, 1)
            V.tensor_scalar(qkw[:, :], par[:, C_QN:C_QN + 1], DH ** -0.5, None, ALU.mult)
            dve.wait_ge(lb_ex, 1)
            link(V.tensor_tensor(small[:, 0:8], lbc[:, 32:40], lbc[:, 40:48], ALU.add))
            link(V.tensor_tensor(small[:, 8:16], small[:, 0:8], lbc[:, 24:32], ALU.add))
            link(V.reciprocal(small[:, 16:24], small[:, 8:16]))
            V.tensor_tensor(lbc[:, 0:8], lbc[:, 24:32], small[:, 16:24], ALU.mult)
            link(V.tensor_tensor(lbc[:, 8:16], small[:, 0:8], small[:, 16:24], ALU.mult))

            def first_dots(k):
                dve.wait_ge(modf_in[k], 16)
                for m in (k, KT + k) if k < SHARED else (k,):
                    ins = V.tensor_tensor_reduce(out=modf[:, m, :], in0=modf[:, m, :], in1=cb[:, :], scale=1.0,
                                                 scalar=0.0, op0=ALU.mult, op1=ALU.add, accum_out=mod[:, m:m + 1])
                link(ins)
                if k >= SHARED:
                    dve.wait_ge(scale_sum, k + 1 - SHARED)
                for m in (k, KT + k):
                    ins = V.tensor_tensor(mod[:, m:m + 1], mod[:, m:m + 1], par[:, C_BMOD + m:C_BMOD + m + 1], ALU.add)
                link(ins)
                link(V.scalar_tensor_tensor(out=gain[:, k:k + 1], in0=mod[:, SC1 + k:SC1 + k + 1], scalar=1.0,
                                            in1=par[:, C_N1 + k:C_N1 + k + 1], op0=ALU.add, op1=ALU.mult))

            link(V.memset(acc[:, :], 0.0))
            for k in range(KT - 1):
                dve.wait_ge(x_sq, k + 1)
                if k:
                    dve.wait_ge(x_acc, k)
                V.tensor_tensor(acc[:, :], acc[:, :], (sqb, scr[0])[k % 2][:, :], ALU.add).then_inc(x_acc, 1)
            dve.wait_ge(cact, 1)
            first_dots(0)
            dve.wait_ge(n_sum, 1)
            eps_var(NORM_BANKS[0][0][:, 0:TT], TT).then_inc(n_var, 1)
            V.memset(acc[:, :], 0.0).then_inc(x_acc, 1)
            first_dots(1)
            dve.wait_ge(n_bc, 1)
            dve.wait_ge(masked, 1)
            t_of(0, 0, 0)
            for k in range(KT):
                if k + 1 < KT:
                    if k:
                        first_dots(k + 1)
                    t_of(0, k + 1, 0)
                lower(0, k, h0, SH1)

            def hg_dense(s, b):
                n, g, j = 6 + 8 * s + b, s + 1, b % 2
                if b in (4, 5):
                    at = 2 * (g % 2) + j
                    dve.wait_ge(ev_f, 2 * g + j + 1)
                    c = 2 * g + j
                    V.tensor_scalar(hf[:, at, :], hf[:, at, :], lbc[:, 8 + c:9 + c], lbc[:, c:c + 1],
                                    ALU.mult, ALU.add)
                    V.tensor_scalar(hk[:, at, :], hk[:, at, :], lbc[:, 8 + c:9 + c], None, ALU.mult).then_inc(kf, 1)
                modulation(n // 4, n % 4)

            def hg_core(s, slot):
                p0 = 2 * (s % 2)
                lv, m = slot, 1 << max(slot - 1, 0)
                for j in range(GH):
                    q, f = hq[:, p0 + j, :], hf[:, p0 + j, :]
                    if slot < SPLITS - 1:
                        dve.wait_ge(lvl, 20 * s + 2 * lv + j + 1)
                        bank = ps[j][:, :].rearrange("p (t q) -> p t q", q=P)
                        ad = adiag[:, j, :].rearrange("p (t q) -> p t q", q=P)
                        if lv == 0:
                            V.tensor_tensor(q, q, f, ALU.mult).then_inc(qup, 1)
                            V.tensor_tensor(ad, bank, ident[:, :].unsqueeze(1).broadcast_to([P, TT, P]),
                                            ALU.mult).then_inc(sel, 1)
                            continue
                        qv = q.rearrange("p (b h m) -> p b h m", h=2, m=m)
                        tv = f.rearrange("p (b h m) -> p b h m", h=2, m=m)
                        V.tensor_tensor(qv[:, :, 1, :], qv[:, :, 1, :],
                                        tv[:, :, 0, 0:1].broadcast_to([P, T // (2 * m), m]), ALU.mult).then_inc(qup, 1)
                        if lv < MASKED:
                            nb = P // (2 * m)
                            mask = second_halves(masks[:, lv, :], m).unsqueeze(1).broadcast_to([P, TT, nb, m])
                            V.copy_predicated(
                                second_halves(adiag[:, j, :], m).rearrange("p (t b) m -> p t b m", b=nb), mask,
                                second_halves(ps[j][:, :], m).rearrange("p (t b) m -> p t b m", b=nb)).then_inc(sel, 1)
                    elif slot == 10:
                        dve.wait_ge(o_ev, 2 * s + j + 1)
                        dve.wait_ge(ev_g, 2 * s + j + 1)
                        V.tensor_tensor(hgate[:, j, :], hgate[:, j, :], q, ALU.mult).then_inc(hgo, 1)
                if slot == 11:
                    dve.wait_ge(g_sum, s + 1)
                    eps_var(ps[0][:, 0:4 * GH], 4 * GH).then_inc(g_var, 1)
                elif slot == 12:
                    for j in range(GH):
                        dve.wait_ge(g_bc, 2 * s + j + 1)
                        dve.wait_ge(hgo, 2 * s + j + 1)
                        if s:
                            dve.wait_ge(y_lo, 2 * s + j - 1)
                        V.scalar_tensor_tensor(out=scr[j][:, :], in0=hgate[:, j, :], scalar=par[:, C_GN:C_GN + 1],
                                               in1=ps[1 + 2 * j][:, :], op0=ALU.mult, op1=ALU.mult).then_inc(y_t, 1)
                    for j in range(GH):
                        half_y(2 * s + j, scr[j], y_hi, y_lo, y0)

            for b in range(2, 8):
                hg_dense(-1, b)
            for s in range(GROUPS):
                for slot in range(len(ENDS[s])):
                    hg_core(s, slot)
                    for s_, b in ended(s, slot, ENDS):
                        hg_dense(s_, b)

            def residual(quads, q0, per, gate, upd0, start_at, rooted):
                dve.wait_ge(x_acc, upd0 + KT)
                link(V.memset(acc[:, :], 0.0))

                def body(q, last):
                    for j in range(0, 4, per):
                        n = q * (4 // per) + j // per
                        dve.wait_ge(pe_blk, (q + q0) * 4 + j + per)
                        V.scalar_tensor_tensor(out=tile(x, n), in0=ps[4 + j // per][:, :], scalar=col(mod, n + gate),
                                               in1=tile(x, n), op0=ALU.mult, op1=ALU.add).then_inc(x_upd, 1)
                        if per == 2 and start_at is not None:
                            for s in range(2):
                                modulation(q + start_at, j + s)
                        if last and rooted and j + per == 4:
                            return
                        dve.wait_ge(x_sq, n + (upd0 + KT + 1))
                        dve.wait_ge(x_acc, n + (upd0 + KT))
                        V.tensor_tensor(acc[:, :], acc[:, :], sqb[:, :], ALU.add).then_inc(x_acc, 1)

                with dve.Fori(0, quads - 1) as q:
                    body(q, False)
                body(quads - 1, True)

            def last_gains():
                dve.wait_ge(mod_set, 20)
                add_bias(48, 96)
                gains(2, C_N1 + 8, 48 + SC1)
                gains(3, C_N2 + 8, 48 + SC2)
                dve.wait_ge(f_w, 1)
                V.tensor_tensor(wfs[1][:, :], wf[:, :], wfs[0][:, :].bitcast(F32), ALU.subtract).then_inc(f_wl, 1)

            def mlp(layer, a, gate, upd0):
                base = layer * LAYER_QUADS + Q_MLP
                for half in range(2):
                    with dve.Fori(0, 4) as q:
                        for j in range(4):
                            n = q * 4 + (32 * layer + 16 * half + j)
                            dve.wait_ge(ff_r, n + 1)
                            V.tensor_tensor(scr[j % 2][:, :], scr[j % 2][:, :], scr[j % 2][:, :], ALU.mult).then_inc(ff_sq, 1)
                            if layer == 0:
                                modulation(q + 8 + 8 * half, j)
                            dve.wait_ge(ff_hi, n + 1)
                            V.tensor_tensor(tile(a[1], q * 4 + j), scr[j % 2][:, :], tile(a[0], q * 4 + j).bitcast(F32),
                                            ALU.subtract).then_inc(ff_lo, 1)
                    if layer == 0 and half:
                        last_gains()
                    residual(4, base + 8 * half + 4, 2, gate, upd0 + KT * half,
                             12 if layer == 0 and half == 0 else None, half == 1)

            dve.wait_ge(mod_set, 8)
            add_bias(16, 48)
            gains(1, C_N2, SC2)
            residual(2, Q_OUT, 1, G1, 0, None, True)
            norm(1, h1, KT, SH2)
            mlp(0, a0, G2, KT)
            norm(2, h2, 2 * KT, 48 + SH1)
            dve.wait_ge(f_pe, 1)
            link(V.memset(prob[:, 0, :], 1.0))
            dve.wait_ge(ac, 1)
            link(V.tensor_scalar(scr[0][:, :], ps[0][:, :], par[:, C_BF:C_BF + 1], 0.0, ALU.add, ALU.min))
            dve.wait_ge(f_ln, 1)
            link(V.tensor_tensor(scr[1][:, :], gs[:, 0, :], scr[0][:, :], ALU.subtract))
            V.tensor_tensor_scan(out=gs[:, 1, :], data0=prob[:, 0, :], data1=scr[1][:, :], initial=0.0,
                                 op0=ALU.mult, op1=ALU.add).then_inc(f_out, 1)
            def sums(g, w):
                for i in range(2):
                    dve.wait_ge(fx_q, 4 * g + 2 * w + i + 1)
                    V.tensor_reduce(out=ssq[:, 16 * w + 8 * i:16 * w + 8 * i + 8],
                                    in_=(sqb, acc)[i][:, :].rearrange("p (a d) -> p a d", d=DH), axis=AX.X,
                                    op=ALU.add).then_inc(fss, 1)
                dve.wait_ge(fss, 4 * g + 2 * w + 2)
                V.tensor_scalar(ssq[:, 16 * w:16 * w + 16], ssq[:, 16 * w:16 * w + 16], 1.0 / DH, EPS,
                                ALU.mult, ALU.add).then_inc(f_var, 1)

            def normed(g, w):
                dve.wait_ge(f_rst, 2 * g + w + 1)
                for i in range(2):
                    v = qkt[w][:, 2 * i:2 * i + 2, :].rearrange("p t (a d) -> p (t a) d", d=DH)
                    V.tensor_tensor(v, v, rst[:, 16 * w + 8 * i:16 * w + 8 * i + 8].unsqueeze(2).broadcast_to([P, 8, DH]),
                                    ALU.mult).then_inc(f_nrm, 1)

            def scored(c):
                dve.wait_ge(s_pe, c + 1)
                if c >= 2:
                    dve.wait_ge(s_p, c - 1)

            def biased(s, u):
                a, i = divmod(u, TT)
                n, c = P * (i + 1), UNITS * s + u
                V.tensor_tensor_reduce(out=scr[u % 2][:, 0:n], in0=ps[bank_of(s, u, 0)][:, 0:n],
                                       in1=fb[:, FH * (s % 2) + a, 0:n], scale=-1.0, scalar=3e38,
                                       op0=ALU.add, op1=ALU.min, accum_out=small[:, c:c + 1]).then_inc(s_ns, 1)

            def turned(s, u):
                n, c = P * (u % TT + 1), UNITS * s + u
                dve.wait_ge(s_tr, c + 1)
                if c >= 2:
                    dve.wait_ge(s_pv, c - 1)
                V.tensor_copy(pT[:, u % 2, 0:n], ps[bank_of(s, u, 1)][:, 0:n]).then_inc(s_pt, 1)

            def head_out(s, a):
                c = UNITS * s + TT * a
                dve.wait_ge(s_pv, c + TT)
                V.reciprocal(rst[:, 32 + 4 * a:36 + 4 * a], den[:, c:c + TT]).then_inc(s_rd, 1)
                dve.wait_ge(s_rd, FH * s + a + 1)
                if s and a == 0:
                    dve.wait_ge(ot_tr, 2 * s)
                V.tensor_tensor(ot[:, :, DH * a:DH * a + DH],
                                ps[2][:, 0:TT * DH].rearrange("p (t d) -> p t d", d=DH),
                                rst[:, 32 + 4 * a:36 + 4 * a].unsqueeze(2).broadcast_to([P, TT, DH]),
                                ALU.mult).then_inc(s_o, 1)

            def gated(s):
                for f in range(2):
                    dve.wait_ge(ot_tr, 2 * s + f + 1)
                    dve.wait_ge(fx_g, 2 * s + 2)
                    V.tensor_tensor((acc, sqb)[f][:, :], ps[2 + f][:, :], gs[:, f, :], ALU.mult).then_inc(fy_t, 1)

            def y_lower(s):
                for f in range(2):
                    half_y(2 * s + f, (acc, sqb)[f], fy_hi, fy_lo, y1)

            for w in range(2):
                sums(0, w)
                normed(0, w)
            def first_biased(s):
                dve.wait_ge(f_bc[s % 2], 16 * (s // 2 + 1))
                scored(UNITS * s)
                V.memset(dots[:, 0:1], 0.0)
                biased(s, 0)

            first_biased(0)
            for s in range(GROUPS):
                for u in range(UNITS):
                    if u + 1 < UNITS:
                        scored(UNITS * s + u + 1)
                        V.memset(dots[:, (u + 1) % 4:(u + 1) % 4 + 1], 0.0)
                        biased(s, u + 1)
                    turned(s, u)
                    if s and u == 0:
                        gated(s - 1)
                    if s and u == 1:
                        y_lower(s - 1)
                    if u % TT == 1 and u > TT:
                        head_out(s, u // TT - 1)
                    if s + 1 < GROUPS:
                        for w in range(2):
                            if u == 8 + 4 * w:
                                sums(s + 1, w)
                            if u == 10 + 4 * w:
                                normed(s + 1, w)
                if s + 1 < GROUPS:
                    first_biased(s + 1)
                head_out(s, FH - 1)
            gated(GROUPS - 1)
            y_lower(GROUPS - 1)
            dve.wait_ge(fy_lo, KT)
            residual(2, LAYER_QUADS + Q_OUT, 1, 48 + G1, 3 * KT, None, True)
            norm(3, h3, 3 * KT, 48 + SH2)
            mlp(1, a1, 48 + G2, 4 * KT)
            root_of_x(4)
            for k in range(KT):
                V.scalar_tensor_tensor(out=x[:, k, :], in0=x[:, k, :], scalar=par[:, C_FIN + k:C_FIN + k + 1],
                                       in1=ps[7][:, :], op0=ALU.mult, op1=ALU.mult).then_inc(out_t_ready, 1)


_INS = ("x_t", "c_row", "stream", "mod_rows", "w_forget", "params")


def _laid_out(i):
    def feature_block(w, n):
        return w[:, P * n:P * n + P].reshape(KT, P, P).transpose(1, 0, 2).reshape(P, D)

    def token_blocks(w, c0):
        part = w[:, c0:c0 + GW].reshape(2, 4, P, GW).transpose(0, 2, 1, 3)
        return list(part.reshape(2, P, D))

    hg_in, fox_in = i["hg_w_in"][0], i["fox_w_in"][0]
    blocks = []
    for layer in range(2):
        def gate_blocks(g):
            w = (hg_in, fox_in)[layer]
            return [feature_block(w, 24 + 2 * g + j) for j in range(2)]

        for g in range(GROUPS):
            if g:
                blocks += gate_blocks(g - 1)
            if layer == 0:
                for part in (0, 1):
                    blocks += [feature_block(hg_in, 8 * part + 2 * g + j) for j in range(2)]
                blocks += token_blocks(hg_in, 2 * D + GW * g)
            else:
                for part in range(3):
                    blocks += token_blocks(fox_in, D * part + GW * g)
        blocks += gate_blocks(GROUPS - 1)
        w_out = i["hg_w_out" if layer == 0 else "fox_w_out"][0]
        blocks += [feature_block(w_out, n) for n in range(KT)]
        w1, w2 = i["mlp_w1"][layer], i["mlp_w2"][layer]
        for half in range(2):
            blocks += [feature_block(w1, HALF * half + n) for n in range(HALF)]
            for n in range(KT):
                for s in range(2):
                    k0 = D * (2 * half + s)
                    blocks.append(feature_block(w2[k0:k0 + D], n))
    stream = np.stack(blocks)
    mod_rows = np.ascontiguousarray(i["w_mod"].transpose(0, 2, 1)).reshape(2 * 48, P, D)
    gate = np.zeros((D, P), np.float32)
    gate[:, 0:HEADS] = fox_in[:, 4 * D:]

    def columns(v):
        return v.reshape(-1, P).T

    bias = np.zeros((P, 1), np.float32)
    bias[0:HEADS, 0] = i["fox_b_f"][0]
    twice = [np.concatenate([i[n][0], i[n][0]])[:, None] for n in ("fox_qn_w", "fox_kn_w")]
    params = np.concatenate(
        [columns(i["norm1_w"].reshape(-1)), columns(i["norm2_w"].reshape(-1)), columns(i["final_w"]),
         columns(i["hg_lb"].reshape(-1)), i["hg_gn_w"][0][:, None], *twice, bias,
         columns(i["b_mod"].reshape(-1))], axis=1)
    x_t = np.ascontiguousarray(i["x"][0].T).reshape(KT, P, T).transpose(1, 0, 2)
    return {"x_t": x_t, "c_row": i["c"], "stream": stream, "mod_rows": mod_rows,
            "w_forget": feature_block(gate, 0), "params": params}


def kernel(**inputs):
    import concourse.bacc as bacc
    from concourse.bass_utils import run_bass_kernel_spmd

    laid = _laid_out({n: np.asarray(a) for n, a in inputs.items()})
    nc = bacc.Bacc("TRN2", target_bir_lowering=False, num_devices=1)
    arrays, args = {}, []
    for name in _INS:
        arrays[name] = np.ascontiguousarray(laid[name])
        args.append(nc.dram_tensor(name, arrays[name].shape, F32, kind="ExternalInput").ap())
    args.append(nc.dram_tensor("out_t", (P, KT, T), F32, kind="ExternalOutput").ap())
    build(nc, *args)
    r = run_bass_kernel_spmd(nc, [arrays], core_ids=[0])
    got = np.asarray(r.results[0]["out_t"])
    return np.ascontiguousarray(got.transpose(2, 1, 0).reshape(1, T, D))
```
